# Optimizing a Trainium2 kernel written in Bass

```python
import numpy as np
import jax, jax.numpy as jnp
from jax import lax

D_MODEL = 2048
BATCH = 1
SEQ = 256
DEPTH = 1

CHUNK = 64
D_MIX = D_MODEL
D_A = D_MIX // 2
D_B = D_MIX // 4
D_C = D_MIX - D_A - D_B
CONV_A = 3
GMLP_BLOCK = 128
HEADS_B = 4
HEAD_DIM_B = D_B // HEADS_B
CONV_C = 31
D_IN = 3 * D_A + 2 * D_B + 2 * D_C
N_EXPERTS = 32
N_GROUPS = 8
EXPERTS_PER_GROUP = N_EXPERTS // N_GROUPS
TOP_K = 2
D_EXPERT = D_MODEL // 4
MOE_BLOCK = 256
LN_EPS = 1e-5
DEEPNORM_ALPHA = (2 * DEPTH) ** 0.25
DEEPNORM_BETA = (8 * DEPTH) ** -0.25

kernel_name = "hybrid_conv_gmlp_conformer_grouped_moe_deepnorm"

def layer_norm(x, g, b):
    xf = x.astype(jnp.float32)
    mu = jnp.mean(xf, axis=-1, keepdims=True)
    var = jnp.mean(jnp.square(xf - mu), axis=-1, keepdims=True)
    y = (xf - mu) * lax.rsqrt(var + LN_EPS) * g.astype(jnp.float32) + b.astype(jnp.float32)
    return y.astype(x.dtype)

def causal_dwconv(x, w):
    k, c = w.shape
    return lax.conv_general_dilated(
        x, w[:, None, :].astype(x.dtype), window_strides=(1,), padding=[(k - 1, 0)],
        dimension_numbers=("NWC", "WIO", "NWC"), feature_group_count=c)

def spatial_mask(dtype):
    pos = np.arange(GMLP_BLOCK) // CHUNK
    return jnp.asarray(pos[None, :] <= pos[:, None], dtype=dtype)

def hybrid_mixer(x, w_in, conv_a, gate_ws, gate_bs, ln_v_g, ln_v_b,
                 conv_c, conv_c_b, ln_c_g, ln_c_b, w_out):
    bsz, seq, _ = x.shape
    h = jnp.einsum("bsd,de->bse", x, w_in)
    cuts = [int(c) for c in np.cumsum([D_A, D_A, D_A, D_B, D_B, D_C])]
    b_gate, c_gate, xa, u, v, ca, cg = jnp.split(h, cuts, axis=-1)
    y_a = b_gate * causal_dwconv(c_gate * xa, conv_a)
    vn = layer_norm(v, ln_v_g, ln_v_b)
    vb = vn.reshape(bsz, seq // GMLP_BLOCK, GMLP_BLOCK, HEADS_B, HEAD_DIM_B)
    ws = gate_ws * spatial_mask(gate_ws.dtype)[None]
    z = jnp.einsum("hij,bnjhd->bnihd", ws, vb) + gate_bs.T[None, None, :, :, None]
    y_b = u * z.reshape(bsz, seq, D_B)
    glu = ca * jax.nn.sigmoid(cg)
    y_c = causal_dwconv(glu, conv_c) + conv_c_b
    y_c = jax.nn.silu(layer_norm(y_c, ln_c_g, ln_c_b))
    y = jnp.concatenate([y_a, y_b, y_c], axis=-1)
    return jnp.einsum("bse,ed->bsd", y, w_out)

def grouped_moe(x, w_router, b_router, w1, w3, w2):
    bsz, seq, d = x.shape
    xt = x.reshape(-1, d)
    t = xt.shape[0]
    s = jax.nn.sigmoid(jnp.einsum("td,de->te", xt.astype(jnp.float32),
                                  w_router.astype(jnp.float32)))
    sel = (s + b_router.astype(jnp.float32)).reshape(t, N_GROUPS, EXPERTS_PER_GROUP)
    group_score = lax.top_k(sel, TOP_K)[0].sum(-1)
    g_idx = jnp.argmax(group_score, axis=-1)
    cand = jnp.take_along_axis(sel, g_idx[:, None, None], axis=1)[:, 0]
    _, local = lax.top_k(cand, TOP_K)
    e_idx = g_idx[:, None] * EXPERTS_PER_GROUP + local
    s_sel = jnp.take_along_axis(s, e_idx, axis=1)
    gates = s_sel / jnp.sum(s_sel, axis=-1, keepdims=True)
    m = t * TOP_K
    flat_e = e_idx.reshape(m)
    flat_t = jnp.arange(m, dtype=jnp.int32) // TOP_K
    flat_g = gates.reshape(m)
    order = jnp.argsort(flat_e)
    se = flat_e[order]
    counts = jnp.bincount(flat_e, length=N_EXPERTS)
    padded = (counts + MOE_BLOCK - 1) // MOE_BLOCK * MOE_BLOCK
    pend = jnp.cumsum(padded)
    pstart = pend - padded
    start = jnp.cumsum(counts) - counts
    dest = pstart[se] + jnp.arange(m) - start[se]
    n_blocks = -(-m // MOE_BLOCK) + N_EXPERTS
    p = n_blocks * MOE_BLOCK
    slot_t = jnp.full((p,), t, jnp.int32).at[dest].set(flat_t[order])
    slot_g = jnp.zeros((p,), jnp.float32).at[dest].set(flat_g[order])
    blk_e = jnp.minimum(jnp.searchsorted(pend, jnp.arange(n_blocks) * MOE_BLOCK, side="right"),
                        N_EXPERTS - 1)
    x_pad = jnp.concatenate([xt, jnp.zeros((1, d), xt.dtype)], axis=0)

    def expert_block(args):
        tok, e = args
        xb = x_pad[tok]
        hb = jax.nn.silu(xb @ w1[e]) * (xb @ w3[e])
        return hb @ w2[e]

    y_slots = lax.map(expert_block, (slot_t.reshape(n_blocks, MOE_BLOCK), blk_e))
    y_slots = y_slots.reshape(p, d) * slot_g[:, None].astype(y_slots.dtype)
    y = jax.ops.segment_sum(y_slots, slot_t, num_segments=t + 1)[:t]
    return y.reshape(bsz, seq, d)

def setup_inputs(seed: int = 0) -> dict:
    key = jax.random.key(seed)
    ks = jax.random.split(key, 24)
    L, D, E, F = DEPTH, D_MODEL, N_EXPERTS, D_EXPERT
    nrm = lambda k, shape, scale: jax.random.normal(k, shape, jnp.float32) * scale
    return {
        "x": nrm(ks[0], (BATCH, SEQ, D), 1.0),
        "ln_in_g": 1.0 + nrm(ks[1], (D,), 0.02),
        "ln_in_b": nrm(ks[2], (D,), 0.02),
        "w_in": nrm(ks[3], (L, D, D_IN), D ** -0.5),
        "conv_a": nrm(ks[4], (L, CONV_A, D_A), CONV_A ** -0.5),
        "gate_ws": nrm(ks[5], (L, HEADS_B, GMLP_BLOCK, GMLP_BLOCK), GMLP_BLOCK ** -0.5),
        "gate_bs": 1.0 + nrm(ks[6], (L, HEADS_B, GMLP_BLOCK), 0.1),
        "ln_v_g": 1.0 + nrm(ks[7], (L, D_B), 0.02),
        "ln_v_b": nrm(ks[8], (L, D_B), 0.02),
        "conv_c": nrm(ks[9], (L, CONV_C, D_C), CONV_C ** -0.5),
        "conv_c_b": nrm(ks[10], (L, D_C), 0.02),
        "ln_c_g": 1.0 + nrm(ks[11], (L, D_C), 0.02),
        "ln_c_b": nrm(ks[12], (L, D_C), 0.02),
        "w_out": nrm(ks[13], (L, D_MIX, D), DEEPNORM_BETA * D_MIX ** -0.5),
        "ln1_g": 1.0 + nrm(ks[14], (L, D), 0.02),
        "ln1_b": nrm(ks[15], (L, D), 0.02),
        "w_router": nrm(ks[16], (D, E), D ** -0.5),
        "b_router": nrm(ks[17], (E,), 0.01),
        "w1": nrm(ks[18], (L, E, D, F), D ** -0.5),
        "w3": nrm(ks[19], (L, E, D, F), D ** -0.5),
        "w2": nrm(ks[20], (L, E, F, D), DEEPNORM_BETA * F ** -0.5),
        "ln2_g": 1.0 + nrm(ks[21], (L, D), 0.02),
        "ln2_b": nrm(ks[22], (L, D), 0.02),
    }

def reference(x, ln_in_g, ln_in_b, w_in, conv_a, gate_ws, gate_bs, ln_v_g, ln_v_b,
              conv_c, conv_c_b, ln_c_g, ln_c_b, w_out, ln1_g, ln1_b,
              w_router, b_router, w1, w3, w2, ln2_g, ln2_b):
    h = layer_norm(x, ln_in_g, ln_in_b)
    for l in range(DEPTH):
        mix = hybrid_mixer(h, w_in[l], conv_a[l], gate_ws[l], gate_bs[l], ln_v_g[l], ln_v_b[l],
                           conv_c[l], conv_c_b[l], ln_c_g[l], ln_c_b[l], w_out[l])
        h = layer_norm(DEEPNORM_ALPHA * h + mix, ln1_g[l], ln1_b[l])
        ffn = grouped_moe(h, w_router, b_router, w1[l], w3[l], w2[l])
        h = layer_norm(DEEPNORM_ALPHA * h + ffn, ln2_g[l], ln2_b[l])
    return h


_drawn_inputs = setup_inputs


def setup_inputs(seed=0):
    import zlib

    import numpy as np

    out = dict(_drawn_inputs(seed))
    spreads = {}
    factors = {'ln_v_g': 8.0,
     'ln_v_b': 14.447,
     'conv_c_b': 3.38,
     'ln_c_g': 13.762,
     'ln_c_b': 8.0,
     'ln2_g': 7.641,
     'ln2_b': 7.818}
    for name, (base, spread) in spreads.items():
        noise = np.random.default_rng([zlib.crc32(name.encode()), seed]).standard_normal(out[name].shape)
        drawn = base * np.exp(spread * noise) if base else spread * noise
        out[name] = __import__('jax').numpy.asarray(drawn.astype(out[name].dtype))
    for name, factor in factors.items():
        out[name] = (out[name] * factor).astype(out[name].dtype)
    return out
```

```python
from contextlib import ExitStack

import concourse.bass as bass
from concourse import mybir

P = 128
F32 = mybir.dt.float32
I32 = mybir.dt.int32
ALU = mybir.AluOpType
ACT = mybir.ActivationFunctionType
AX_X = mybir.AxisListType.X
EPS = 1e-5
ALPHA = 2.0 ** 0.25
FAR = 1e30


def hybrid_layer(nc, x, ln_in_g, ln_in_b, w_in, conv_a, gate_ws, gate_bs, ln_v_g, ln_v_b,
                 conv_c, conv_c_b, ln_c_g, ln_c_b, w_out, ln1_g, ln1_b, w_router, b_router,
                 w1, w3, w2, ln2_g, ln2_b, out):
    _, SEQ, D = x.shape
    TT = SEQ // P
    KT = D // P
    TAPS_A, D_A = conv_a.shape[1:]
    TAPS_C, D_C = conv_c.shape[1:]
    HEADS = gate_ws.shape[1]
    BLK = gate_ws.shape[2]
    D_B = ln_v_g.shape[1]
    E = w_router.shape[1]
    FE = w1.shape[3]
    FT = FE // P
    CW = 512
    CT = CW // P
    NG, GE = 8, 4
    CAP = 64
    BLOCKS = SEQ // CAP
    PAIRS = E // 2
    NC = D // CW
    N_IN = w_in.shape[2] // CW
    N_OUT = NC
    N_MIX = N_IN + N_OUT
    STEP_CHUNKS = 6
    RING = 3
    HALF = KT // 2
    ROW_A = TAPS_C + 3
    ROWS = ROW_A + 2 * TAPS_A
    PAD_A, PAD_C = TAPS_A - 1, TAPS_C - 1
    assert TT == 2 and BLK == P and D_A == 2 * CW and D_B == D_C == CW and HEADS == CT
    assert (N_MIX + STEP_CHUNKS) % RING == N_MIX % RING

    B0, C0, XA0 = 0, D_A, 2 * D_A
    U0 = 3 * D_A
    V0, CA0, CG0 = U0 + D_B, U0 + 2 * D_B, U0 + 2 * D_B + D_C
    in_cols = [CA0, CG0, V0, U0] + [c + h * CW for h in range(2) for c in (C0, XA0, B0)]
    N_FIRST = 4
    assert len(in_cols) == N_IN

    with ExitStack() as ctx:
        def sb(name, shape, dt=F32):
            return ctx.enter_context(nc.sbuf_tensor(name, shape, dt))

        def sem(name):
            return ctx.enter_context(nc.semaphore(name))

        ring = sb("ring", [P, RING, 2, HALF * CW])
        area_a = sb("area_a", [P, TT, D])
        area_b = sb("area_b", [P, TT, D])
        area_c = sb("area_c", [P, KT, SEQ])
        area_d = sb("area_d", [P, KT, SEQ])
        area_g = sb("area_g", [P, 2, D])
        psum = ctx.enter_context(nc.psum_tensor("psum", [P, 8, CW], F32))

        flat_a = area_a[:].rearrange("p t d -> p (t d)")
        flat_g = area_g[:].rearrange("p t d -> p (t d)")

        def quarter(flat, n):
            return flat[:, n * CT * SEQ:(n + 1) * CT * SEQ]

        plain = quarter(flat_a, 0).rearrange("p (c s) -> p c s", c=CT)
        sigm = quarter(flat_a, 1).rearrange("p (c s) -> p c s", c=CT)
        work = quarter(flat_a, 2).rearrange("p (c s) -> p c s", c=CT)
        v_rows = quarter(flat_a, 3).rearrange("p (k c) -> p k c", k=2)
        u_cm = quarter(flat_g, 0).rearrange("p (c s) -> p c s", c=CT)
        v_tm = quarter(flat_g, 1).rearrange("p (t c) -> p t c", t=TT)
        yc = quarter(flat_g, 2).rearrange("p (c s) -> p c s", c=CT)
        gate_shift = quarter(flat_g, 3)[:, 0:HEADS * BLK].rearrange("p (h i) -> p h i", h=HEADS)

        glu = sb("glu", [P, CT, PAD_C + SEQ])
        gated_x = sb("gated_x", [P, CT, PAD_A + SEQ])
        rows = sb("rows", [ROWS, CW])
        chan = sb("chan", [P, CT, ROWS])
        ws_raw = sb("ws_raw", [P, HEADS, BLK])
        ws_t = sb("ws_t", [P, HEADS, BLK])
        ident = sb("ident", [P, P])
        ones = sb("ones", [P, P])
        mean_w = sb("mean_w", [P, P])
        before = sb("before", [P, P])
        slot_no = sb("slot_no", [P, 2 * TT, CAP])
        group_key = sb("group_key", [P, TT, NG])
        expert_key = sb("expert_key", [P, TT, E])
        w_rt = sb("w_rt", [P, KT, E])
        b_rt = sb("b_rt", [P, E])
        stats = sb("stats", [P, TT, NC, 6])
        mv = sb("mv", [P, TT, 2])
        rstd = sb("rstd", [P, TT, 3])
        v_stats = sb("v_stats", [P, TT, 6])
        c_rstd = sb("c_rstd", [P, 2, SEQ])
        rank = sb("rank", [P, TT, (BLOCKS + 1) * E])
        gate = sb("gate", [P, TT, (BLOCKS + 1) * E])
        one_hot = sb("one_hot", [P, TT, 2, CAP])
        one_hot_g = sb("one_hot_g", [P, TT, 2, CAP])
        one_hot_gt = sb("one_hot_gt", [P, TT, P])
        overflow = sb("overflow", [P, 1], I32)

        flat_d = area_d[:].rearrange("p k s -> p (k s)")
        y_sb = flat_d[:, 0:D]
        silu_h = flat_d[:, D:D + CW]
        hidden = flat_d[:, D + CW:D + 2 * CW]
        hidden_t = flat_d[:, D + 2 * CW:D + 3 * CW].rearrange("p (f s) -> p f s", f=FT)
        rt = flat_d[:, D + 3 * CW:D + 4 * CW].rearrange("p (n w) -> p n w", w=TT * E)
        gathered = area_c[:].rearrange("p k s -> p (k s)")[:, 0:KT * P].rearrange("p (k s) -> p k s", k=KT)

        s_x, s_small, s_ws, s_g, s_vrow, s_out = (
            sem(n) for n in ("x_loaded", "rows_loaded", "ws_loaded", "ln_rows_loaded", "v_rows_loaded", "stored"))
        loaded = [sem(f"chunk_loaded{i}") for i in range(RING)]
        consts = sem("consts_ready")
        chunk_done = sem("chunk_done")
        drained = [sem(f"psum_drained{i}") for i in range(3)]
        extra_ready, extra_drained = sem("extra_ready"), sem("extra_drained")
        dve_step = sem("dve_step")
        var_ready, root_ready = sem("var_ready"), sem("root_ready")
        h0_ready, vn_ready, conv_c_step = sem("h0_ready"), sem("vn_ready"), sem("conv_c_step")
        z_ready, z_used = sem("z_ready"), sem("z_used")
        c_mean, c_sq, c_var, c_varused, c_norm, yc_done = (
            sem(n) for n in ("c_mean_ready", "c_squares_ready", "c_var_ready", "c_var_used", "c_normed", "y_c_done"))
        conv_step = sem("conv_a_step")
        x1_ready, res_ready = sem("x1_ready"), sem("residual_ready")
        logits_ready, probs_ready, picks_ready, ranks_ready = (
            sem(n) for n in ("logits_ready", "probs_ready", "picks_ready", "ranks_ready"))
        flag_ready = sem("flag_ready")
        onehot_ready, gated_ready = sem("onehot_ready"), sem("gated_onehot_ready")
        gather_ready, gather_drained = sem("gather_ready"), sem("gather_drained")
        silu_ready, hidden_ready = sem("silu_ready"), sem("hidden_ready")
        ht_ready, ht_drained = sem("hidden_t_ready"), sem("hidden_t_drained")
        gt_ready, gt_drained = sem("onehot_t_ready"), sem("onehot_t_drained")
        y_ready, y_drained = sem("y_ready"), sem("y_drained")
        comb_ready, comb_added = sem("combined_ready"), sem("combined_added")
        y_out = sem("y_out")

        def chunk_psum(n):
            b = 2 * (n % 3)
            return psum[:, b:b + 2, :]

        def channel_psum(n):
            return chunk_psum(n).rearrange("p b (c s) -> p (b c) s", s=SEQ)

        def spread(row):
            return row.partition_broadcast(P)

        block = ctx.enter_context(nc.Block())

        @block.sync
        def _(sp):
            for t in range(TT):
                sp.dma_start(area_a[:, t, :], x[0, t * P:(t + 1) * P, :]).then_inc(s_x, 16)

            def load_mixer_chunk(n):
                if n >= RING:
                    sp.wait_ge(chunk_done, n - RING + 1)
                if n < N_IN:
                    src = w_in[0][:, in_cols[n]:in_cols[n] + CW]
                else:
                    src = w_out[0][:, (n - N_IN) * CW:(n - N_IN + 1) * CW]
                src = src.rearrange("(h k p) c -> h p k c", h=2, p=P)
                for h in range(2):
                    dst = ring[:, n % RING, h, :].rearrange("p (k c) -> p k c", k=HALF)
                    sp.dma_start(dst, src[h]).then_inc(loaded[n % RING], 16)

            for n in range(N_MIX):
                load_mixer_chunk(n)
                if n == N_MIX - 1:
                    sp.dma_start(area_g[:, 0, :], spread(ln1_g[0])).then_inc(s_g, 16)
                    sp.dma_start(area_g[:, 1, :], spread(ln1_b[0])).then_inc(s_g, 16)

            def load_step(it, pair):
                for j in range(STEP_CHUNKS):
                    slot = (N_MIX + j) % RING
                    sp.wait_ge(chunk_done, STEP_CHUNKS * it + N_MIX + j - RING + 1)
                    for i in range(2):
                        e = 2 * pair + i
                        if j < 4:
                            src = (w1, w3)[j // 2][0, e].rearrange("(h k p) f -> h p k f", h=2, p=P)[j % 2]
                            dst = ring[:, slot, i, :].rearrange("p (k f) -> p k f", k=HALF)
                        else:
                            src = w2[0, e].rearrange("(f p) (h d) -> h p f d", p=P, h=2)[j % 2]
                            dst = ring[:, slot, i, :].rearrange("p (f d) -> p f d", f=FT)
                        sp.dma_start(dst, src).then_inc(loaded[slot], 16)

            with sp.Fori(0, PAIRS) as it:
                load_step(it, it)
            sp.wait_ge(x1_ready, TT)
            sp.dma_start(area_g[:, 0, :], spread(ln2_g[0])).then_inc(s_g, 16)
            sp.dma_start(area_g[:, 1, :], spread(ln2_b[0])).then_inc(s_g, 16)
            sp.wait_ge(flag_ready, 1)
            more = sp.value_load(overflow[0:1, 0:1], min_val=0, max_val=1)
            with sp.If(more > 0):
                with sp.Fori(1, BLOCKS) as b:
                    with sp.Fori(0, PAIRS) as p:
                        load_step(b * PAIRS + p, p)
                sp.nop()
            with sp.Else():
                sp.nop()
            for t in range(TT):
                sp.wait_ge(y_out, t + 1)
                sp.dma_start(out[0, t * P:(t + 1) * P, :], area_b[:, t, :]).then_inc(s_out, 16)
            sp.wait_ge(s_out, 16 * TT)

        @block.gpsimd
        def _(pool):
            nc.gpsimd.memset(ones[:], 1.0).then_inc(consts, 1)
            nc.gpsimd.memset(mean_w[:], 1.0 / D_C).then_inc(consts, 1)
            pool.wait_ge(consts, 1)
            nc.gpsimd.affine_select(out=ident[:], in_=ones[:], compare_op=ALU.is_equal, fill=0.0, base=0,
                                    pattern=[[-1, P]], channel_multiplier=1).then_inc(consts, 1)
            nc.gpsimd.affine_select(out=before[:], in_=ones[:], compare_op=ALU.is_gt, fill=0.0, base=0,
                                    pattern=[[1, P]], channel_multiplier=-1).then_inc(consts, 1)
            nc.gpsimd.iota(slot_no[:], pattern=[[0, 2 * TT], [1, CAP]], base=0, channel_multiplier=0,
                           allow_small_or_imprecise_dtypes=True).then_inc(consts, 1)
            nc.gpsimd.iota(group_key[:], pattern=[[0, TT], [-1, NG]], base=NG, channel_multiplier=0,
                           allow_small_or_imprecise_dtypes=True).then_inc(consts, 1)
            nc.gpsimd.iota(expert_key[:], pattern=[[0, TT], [-1, E]], base=E, channel_multiplier=0,
                           allow_small_or_imprecise_dtypes=True).then_inc(consts, 1)
            nc.gpsimd.memset(glu[:, :, 0:PAD_C], 0.0).then_inc(consts, 1)
            nc.gpsimd.memset(gated_x[:, :, 0:PAD_A], 0.0).then_inc(consts, 1)
            pool.wait_ge(consts, 9)
            nc.gpsimd.memset(ws_t[P // 2:P, :, 0:BLK // 2], 0.0).then_inc(consts, 1)
        CONSTS = 10

        @block.tensor
        def _(pe):
            pe.wait_ge(consts, CONSTS)
            pe.wait_ge(s_small, 16 * 6)
            for c in range(CT):
                mm = pe.transpose(psum[:, 6, c * ROWS:(c + 1) * ROWS], rows[:, c * P:(c + 1) * P],
                                  ident[0:ROWS, 0:ROWS])
            mm.then_inc(extra_ready, 1)
            pe.wait_ge(s_ws, 16)
            for h in range(HEADS):
                mm = pe.transpose(psum[:, 7, h * P:(h + 1) * P], ws_raw[:, h, :], ident[:])
            mm.then_inc(extra_ready, 1)

            def turn_rows(ready, t, first):
                pe.wait_ge(ready, t + 1)
                for g in range(KT // 4):
                    n = first + t * (KT // 4) + g
                    pe.wait_ge(extra_drained, n - 1)
                    for j in range(4):
                        k = 4 * g + j
                        mm = pe.transpose(psum[:, 6 + n % 2, j * P:(j + 1) * P],
                                          area_b[:, t, k * P:(k + 1) * P], ident[:])
                    mm.then_inc(extra_ready, 1)

            for t in range(TT):
                turn_rows(h0_ready, t, 2)
            EX = 2 + TT * KT // 4
            pe.wait_ge(extra_drained, EX)

            def weights(n):
                pe.wait_ge(loaded[n % RING], 32 * (n // RING + 1))
                half = [ring[:, n % RING, h, :].rearrange("p (k c) -> p k c", k=HALF) for h in range(2)]
                return lambda k: half[k // HALF][:, k % HALF, :]

            def channels(n, w):
                o = channel_psum(n)
                for c in range(CT):
                    for k in range(KT):
                        mm = pe.matmul(o[:, c, :], w(k)[:, c * P:(c + 1) * P], area_c[:, k, :],
                                       start=k == 0, stop=k == KT - 1)
                mm.then_inc(chunk_done, 1)

            def tokens(n, w, lhs):
                o = chunk_psum(n)
                for t in range(TT):
                    for k in range(KT):
                        mm = pe.matmul(o[:, t, :], lhs[:, k, t * P:(t + 1) * P], w(k),
                                       start=k == 0, stop=k == KT - 1)
                mm.then_inc(chunk_done, 1)

            channels(0, weights(0))
            channels(1, weights(1))
            tokens(2, weights(2), area_c)
            w = weights(3)
            pe.wait_ge(drained[0], 1)
            channels(3, w)

            pe.wait_ge(conv_c_step, TAPS_C * CT)
            for c in range(CT):
                mm = pe.matmul(psum[:, 6, 0:SEQ], mean_w[:], yc[:, c, :], start=c == 0, stop=c == CT - 1)
            mm.then_inc(c_mean, 1)
            pe.wait_ge(c_sq, 1)
            for c in range(CT):
                mm = pe.matmul(psum[:, 7, 0:SEQ], mean_w[:], work[:, c, :], start=c == 0, stop=c == CT - 1)
            mm.then_inc(c_var, 1)
            pe.wait_ge(vn_ready, 1)
            pe.wait_ge(c_varused, 1)
            z = psum[:, 6:8, :].rearrange("p b (h s) -> p (b h) s", s=SEQ)
            for h in range(HEADS):
                for t in range(TT):
                    mm = pe.matmul(z[:, h, t * P:(t + 1) * P], v_tm[:, t, h * P:(h + 1) * P], ws_t[:, h, :],
                                   start=True, stop=True)
            mm.then_inc(z_ready, 1)

            with pe.Fori(0, 2) as a:
                for j in range(3):
                    n = N_FIRST + j
                    pe.wait_ge(loaded[n % RING], 32 * (n // RING + 1) + 32 * a)
                    pe.wait_ge(drained[n % 3], n // 3 + a)
                    half = [ring[:, n % RING, h, :].rearrange("p (k c) -> p k c", k=HALF) for h in range(2)]
                    channels(n, lambda k: half[k // HALF][:, k % HALF, :])

            pe.wait_ge(z_used, 1)
            pe.wait_ge(yc_done, CT)
            pe.wait_ge(drained[0], 4)
            for c in range(N_OUT):
                n = N_IN + c
                w = weights(n)
                pe.wait_ge(drained[n % 3], n // 3)
                tokens(n, w, area_d)

            for t in range(TT):
                turn_rows(x1_ready, t, EX)
            pe.wait_ge(extra_drained, EX + TT * KT // 4)
            for t in range(TT):
                for k in range(KT):
                    mm = pe.matmul(psum[:, 0, t * E:(t + 1) * E], area_c[:, k, t * P:(t + 1) * P],
                                   w_rt[:, k, :], start=k == 0, stop=k == KT - 1)
            mm.then_inc(logits_ready, 1)
            pe.wait_ge(picks_ready, 1)
            picks = rt[:, 5, :].rearrange("p (t e) -> p t e", t=TT)
            pe.matmul(psum[:, 1, 0:E], before[:], picks[:, 0, :], start=True, stop=True)
            pe.matmul(psum[:, 1, E:2 * E], ones[:], picks[:, 0, :], start=True, stop=False)
            pe.matmul(psum[:, 1, E:2 * E], before[:], picks[:, 1, :], start=False, stop=True)
            pe.matmul(psum[:, 1, 2 * E:3 * E], ones[:], picks[:, 0, :], start=True, stop=False)
            pe.matmul(psum[:, 1, 2 * E:3 * E], ones[:], picks[:, 1, :], start=False, stop=True).then_inc(ranks_ready, 1)

            def gather(it):
                pe.wait_ge(onehot_ready, it + 1)
                for g in range(KT // 4):
                    if g >= 2:
                        pe.wait_ge(gather_drained, 4 * it + g - 1)
                    for j in range(4):
                        k = 4 * g + j
                        for t in range(TT):
                            mm = pe.matmul(psum[:, 2 + g % 2, j * P:(j + 1) * P],
                                           area_b[:, t, k * P:(k + 1) * P],
                                           one_hot[:, t].rearrange("p i s -> p (i s)"),
                                           start=t == 0, stop=t == TT - 1)
                    mm.then_inc(gather_ready, 1)

            def step(it):
                pe.wait_ge(gather_drained, 4 * it + 4)
                for j in range(4):
                    slot = (N_MIX + j) % RING
                    pe.wait_ge(loaded[slot], 64 * it + 32 * ((N_MIX + j) // RING + 1))
                    bank = j // 2
                    for k in range(HALF):
                        kk = (j % 2) * HALF + k
                        for i in range(2):
                            mm = pe.matmul(psum[i * CAP:(i + 1) * CAP, bank, :],
                                           gathered[:, kk, i * CAP:(i + 1) * CAP],
                                           ring[:, slot, i, k * CW:(k + 1) * CW],
                                           start=kk == 0, stop=kk == KT - 1)
                    mm.then_inc(chunk_done, 1)
                gather(it + 1)
                pe.wait_ge(hidden_ready, it + 1)
                pe.wait_ge(gather_drained, 4 * it + 7)
                for f in range(FT):
                    mm = pe.transpose(psum[:, 2, f * P:(f + 1) * P], hidden[:, f * P:(f + 1) * P], ident[:])
                mm.then_inc(ht_ready, 1)
                pe.wait_ge(gated_ready, it + 1)
                pe.wait_ge(gather_drained, 4 * it + 8)
                for t in range(TT):
                    mm = pe.transpose(psum[:, 3, t * P:(t + 1) * P],
                                      one_hot_g[:, t].rearrange("p i s -> p (i s)"), ident[:])
                mm.then_inc(gt_ready, 1)
                pe.wait_ge(ht_drained, it + 1)

                def project(c):
                    j = 4 + c // 2
                    slot = (N_MIX + j) % RING
                    if c % 2 == 0:
                        pe.wait_ge(loaded[slot], 64 * it + 32 * ((N_MIX + j) // RING + 1))
                    if c >= 2:
                        pe.wait_ge(y_drained, 4 * it + c - 1)
                    for f in range(FT):
                        for i in range(2):
                            at = f * (D // 2) + (c % 2) * CW
                            mm = pe.matmul(psum[i * CAP:(i + 1) * CAP, 4 + c % 2, :],
                                           hidden_t[:, f, i * CAP:(i + 1) * CAP],
                                           ring[:, slot, i, at:at + CW], start=f == 0, stop=f == FT - 1)
                    mm.then_inc(y_ready, 1)

                def combine(c):
                    pe.wait_ge(y_drained, 4 * it + c + 1)
                    if c == 0:
                        pe.wait_ge(gt_drained, it + 1)
                    else:
                        pe.wait_ge(comb_added, 4 * it + c)
                    for t in range(TT):
                        mm = pe.matmul(psum[:, 6 + t, :], one_hot_gt[:, t, :], y_sb[:, c * CW:(c + 1) * CW],
                                       start=True, stop=True)
                        if t == 0 and c % 2 == 0:
                            mm.then_inc(chunk_done, 1)
                    mm.then_inc(comb_ready, 1)

                project(0)
                project(1)
                combine(0)
                project(2)
                combine(1)
                project(3)
                combine(2)
                combine(3)

            gather(0)
            with pe.Fori(0, PAIRS) as it:
                step(it)
            pe.wait_ge(flag_ready, 1)
            more = pe.value_load(overflow[0:1, 0:1], min_val=0, max_val=1)
            with pe.If(more > 0):
                with pe.Fori(PAIRS, BLOCKS * PAIRS) as it:
                    step(it)
                pe.nop()
            with pe.Else():
                pe.nop()

        @block.scalar
        def _(act):
            act.dma_start(rows[0:TAPS_C, :], conv_c[0]).then_inc(s_small, 16)
            for r, src in enumerate((conv_c_b, ln_c_g, ln_c_b)):
                act.dma_start(rows[TAPS_C + r:TAPS_C + r + 1, :], src).then_inc(s_small, 16)
            for h in range(2):
                act.dma_start(rows[ROW_A + h * TAPS_A:ROW_A + (h + 1) * TAPS_A, :],
                              conv_a[0][:, h * CW:(h + 1) * CW]).then_inc(s_small, 16)
            act.dma_start(ws_raw[:], gate_ws[0].rearrange("h i j -> i h j")).then_inc(s_ws, 16)
            act.dma_start(area_g[:, 0, :], spread(ln_in_g)).then_inc(s_g, 16)
            act.dma_start(area_g[:, 1, :], spread(ln_in_b)).then_inc(s_g, 16)
            act.dma_start(w_rt[:], w_router.rearrange("(k p) e -> p k e", p=P)).then_inc(s_vrow, 16)
            act.dma_start(b_rt[:], spread(b_router)).then_inc(s_vrow, 16)

            act.wait_ge(extra_ready, 1)
            act.activation(chan[:], psum[:, 6, 0:CT * ROWS].rearrange("p (c r) -> p c r", c=CT),
                           ACT.Copy).then_inc(extra_drained, 1)
            act.wait_ge(extra_ready, 2)
            wsp = psum[:, 7, :].rearrange("p (h i) -> p h i", h=HEADS)
            act.activation(ws_t[0:P // 2], wsp[0:P // 2], ACT.Copy)
            act.activation(ws_t[P // 2:P, :, BLK // 2:], wsp[P // 2:P, :, BLK // 2:],
                           ACT.Copy).then_inc(extra_drained, 1)

            def root(n):
                act.wait_ge(var_ready, n)
                act.activation(rstd[:, :, 1], rstd[:, :, 0], ACT.Sqrt).then_inc(root_ready, 1)

            def keep_turned(first):
                for n in range(first, first + TT * KT // 4):
                    t, g = divmod(n - first, KT // 4)
                    act.wait_ge(extra_ready, n + 1)
                    act.activation(area_c[:, 4 * g:4 * g + 4, t * P:(t + 1) * P],
                                   psum[:, 6 + n % 2, :].rearrange("p (j s) -> p j s", j=4),
                                   ACT.Copy).then_inc(extra_drained, 1)

            root(1)
            keep_turned(2)
            act.wait_ge(h0_ready, TT)
            act.dma_start(v_rows[:, 0, :], spread(ln_v_g[0])).then_inc(s_vrow, 16)
            act.dma_start(v_rows[:, 1, :], spread(ln_v_b[0])).then_inc(s_vrow, 16)
            act.dma_start(gate_shift, spread(gate_bs[0])).then_inc(s_vrow, 16)

            act.wait_ge(chunk_done, 1)
            act.activation(plain, channel_psum(0), ACT.Copy).then_inc(drained[0], 1)
            act.wait_ge(chunk_done, 2)
            act.activation(sigm, channel_psum(1), ACT.Sigmoid).then_inc(drained[1], 1)
            root(2)
            act.wait_ge(chunk_done, 4)
            act.activation(u_cm, channel_psum(3), ACT.Copy).then_inc(drained[0], 1)
            act.wait_ge(c_varused, 1)
            act.activation(c_rstd[:, 1, :], c_rstd[:, 0, :], ACT.Sqrt).then_inc(root_ready, 1)
            act.wait_ge(c_norm, 1)
            for c in range(CT):
                act.activation(area_d[:, 12 + c, :], yc[:, c, :], ACT.Silu, scale=chan[:, c, TAPS_C + 1:TAPS_C + 2],
                               bias=chan[:, c, TAPS_C + 2:TAPS_C + 3]).then_inc(yc_done, 1)
            with act.Fori(0, 2) as a:
                act.wait_ge(chunk_done, N_FIRST + 1 + 3 * a)
                act.wait_ge(drained[2], 1 + a)
                act.activation(plain, channel_psum(N_FIRST), ACT.Copy).then_inc(drained[1], 1)

            root(3)
            for t in range(TT):
                act.wait_ge(x1_ready, t + 1)
                act.activation(area_a[:, t, :], area_b[:, t, :], ACT.Copy, scale=ALPHA).then_inc(res_ready, 1)
                first = 2 + TT * KT // 4
                for g in range(KT // 4):
                    n = first + t * (KT // 4) + g
                    act.wait_ge(extra_ready, n + 1)
                    act.activation(area_c[:, 4 * g:4 * g + 4, t * P:(t + 1) * P],
                                   psum[:, 6 + n % 2, :].rearrange("p (j s) -> p j s", j=4),
                                   ACT.Copy).then_inc(extra_drained, 1)
            act.wait_ge(logits_ready, 1)
            act.activation(rt[:, 0, :], psum[:, 0, 0:TT * E], ACT.Sigmoid).then_inc(probs_ready, 1)

            def keep_gathered(it):
                for g in range(KT // 4):
                    act.wait_ge(gather_ready, 4 * it + g + 1)
                    act.activation(gathered[:, 4 * g:4 * g + 4, :],
                                   psum[:, 2 + g % 2, :].rearrange("p (j s) -> p j s", j=4),
                                   ACT.Copy).then_inc(gather_drained, 1)

            def step(it):
                act.wait_ge(chunk_done, STEP_CHUNKS * it + N_MIX + 2)
                act.activation(silu_h, psum[:, 0, :], ACT.Silu).then_inc(silu_ready, 1)
                keep_gathered(it + 1)
                act.wait_ge(ht_ready, it + 1)
                act.activation(hidden_t, psum[:, 2, :].rearrange("p (f s) -> p f s", f=FT),
                               ACT.Copy).then_inc(ht_drained, 1)
                act.wait_ge(gt_ready, it + 1)
                act.activation(one_hot_gt[:], psum[:, 3, 0:TT * P].rearrange("p (t s) -> p t s", t=TT),
                               ACT.Copy).then_inc(gt_drained, 1)
                for c in range(NC):
                    act.wait_ge(y_ready, 4 * it + c + 1)
                    act.activation(y_sb[:, c * CW:(c + 1) * CW], psum[:, 4 + c % 2, :],
                                   ACT.Copy).then_inc(y_drained, 1)

            keep_gathered(0)
            with act.Fori(0, PAIRS) as it:
                step(it)
            act.wait_ge(flag_ready, 1)
            more = act.value_load(overflow[0:1, 0:1], min_val=0, max_val=1)
            with act.If(more > 0):
                with act.Fori(PAIRS, BLOCKS * PAIRS) as it:
                    step(it)
                act.nop()
            with act.Else():
                act.nop()
            root(4)

        @block.vector
        def _(dve):
            v = nc.vector
            steps = [0]

            def link(ins):
                steps[0] += 1
                ins.then_inc(dve_step, 1)
                dve.wait_ge(dve_step, steps[0])

            def inverse_root(n):
                v.tensor_scalar(rstd[:, :, 0], mv[:, :, 1], EPS, None, ALU.add).then_inc(var_ready, 1)
                dve.wait_ge(root_ready, n)
                link(v.reciprocal(rstd[:, :, 2], rstd[:, :, 1]))

            def apply_norm(t, src, ready, scaled_by):
                dst = area_b[:, t, :]
                link(v.tensor_scalar(dst, src, mv[:, t, 0:1], rstd[:, t, 2:3], ALU.subtract, ALU.mult))
                if t == 0:
                    dve.wait_ge(s_g, 32 * scaled_by)
                link(v.tensor_tensor(dst, dst, area_g[:, 0, :], ALU.mult))
                v.tensor_tensor(dst, dst, area_g[:, 1, :], ALU.add).then_inc(ready, 1)

            dve.wait_ge(s_x, 16 * TT)
            for t in range(TT):
                for c in range(NC):
                    link(v.bn_stats(stats[:, t, c, :], area_a[:, t, c * CW:(c + 1) * CW]))
                link(v.bn_aggr(mv[:, t, :], stats[:, t]))
            inverse_root(1)
            for t in range(TT):
                apply_norm(t, area_a[:, t, :], h0_ready, 1)

            dve.wait_ge(drained[0], 1)
            dve.wait_ge(drained[1], 1)
            dve.wait_ge(consts, CONSTS)
            dve.wait_ge(extra_drained, 2)
            link(v.tensor_tensor(glu[:, :, PAD_C:], plain, sigm, ALU.mult))
            for k in range(TAPS_C):
                for c in range(CT):
                    if k >= 1:
                        dve.wait_ge(conv_c_step, (k - 1) * CT + c + 1)
                    tap = chan[:, c, k:k + 1]
                    src = glu[:, c, k:k + SEQ]
                    if k == 0:
                        ins = v.tensor_scalar(yc[:, c, :], src, tap, chan[:, c, TAPS_C:TAPS_C + 1],
                                              ALU.mult, ALU.add)
                    else:
                        ins = v.scalar_tensor_tensor(out=yc[:, c, :], in0=src, scalar=tap, in1=yc[:, c, :],
                                                     op0=ALU.mult, op1=ALU.add)
                    ins.then_inc(conv_c_step, 1)
            dve.wait_ge(conv_c_step, TAPS_C * CT)

            dve.wait_ge(chunk_done, 3)
            v_ps = chunk_psum(2)
            for t in range(TT):
                link(v.bn_stats(v_stats[:, t, :], v_ps[:, t, :]))
                link(v.bn_aggr(mv[:, t, :], v_stats[:, t:t + 1, :]))
            inverse_root(2)
            link(v.tensor_scalar(v_tm[:, 0, :], v_ps[:, 0, :], mv[:, 0, 0:1], rstd[:, 0, 2:3],
                                 ALU.subtract, ALU.mult))
            v.tensor_scalar(v_tm[:, 1, :], v_ps[:, 1, :], mv[:, 1, 0:1], rstd[:, 1, 2:3],
                            ALU.subtract, ALU.mult).then_inc(drained[2], 1)
            dve.wait_ge(drained[2], 1)
            dve.wait_ge(s_vrow, 16 * 5)
            link(v.tensor_tensor(v_tm, v_tm, v_rows[:, 0:1, :].to_broadcast([P, TT, CW]), ALU.mult))
            v.tensor_tensor(v_tm, v_tm, v_rows[:, 1:2, :].to_broadcast([P, TT, CW]), ALU.add).then_inc(vn_ready, 1)

            dve.wait_ge(c_mean, 1)
            mean = psum[:, 6:7, 0:SEQ].to_broadcast([P, CT, SEQ])
            link(v.tensor_tensor(yc, yc, mean, ALU.subtract))
            v.tensor_tensor(work, yc, yc, ALU.mult).then_inc(c_sq, 1)
            dve.wait_ge(c_var, 1)
            v.tensor_scalar(c_rstd[:, 0, :], psum[:, 7, 0:SEQ], EPS, None, ALU.add).then_inc(c_varused, 1)
            dve.wait_ge(root_ready, 3)
            link(v.reciprocal(c_rstd[:, 0, :], c_rstd[:, 1, :]))
            v.tensor_tensor(yc, yc, c_rstd[:, 0:1, :].to_broadcast([P, CT, SEQ]), ALU.mult).then_inc(c_norm, 1)

            dve.wait_ge(z_ready, 1)
            z = psum[:, 6:8, :].rearrange("p b (h s) -> p (b h) s", s=SEQ)
            for t in range(TT):
                link(v.tensor_tensor(work[:, :, t * P:(t + 1) * P], z[:, :, t * P:(t + 1) * P], gate_shift, ALU.add))
            dve.wait_ge(drained[0], 2)
            v.tensor_tensor(area_d[:, 8:12, :], work, u_cm, ALU.mult).then_inc(z_used, 1)

            PER = CT * TAPS_A
            with dve.Fori(0, 2) as a:
                dve.wait_ge(chunk_done, N_FIRST + 2 + 3 * a)
                dve.wait_ge(drained[1], 2 + a)
                v.tensor_tensor(gated_x[:, :, PAD_A:], plain, channel_psum(N_FIRST + 1),
                                ALU.mult).then_inc(drained[2], 1)
                dve.wait_ge(drained[2], 2 + a)
                dve.wait_ge(z_used, 1)
                for k in range(TAPS_A):
                    for c in range(CT):
                        if k >= 1:
                            dve.wait_ge(conv_step, PER * a + (k - 1) * CT + c + 1)
                        tap = chan[:, c, bass.ds(TAPS_A * a + (ROW_A + k), 1)]
                        src = gated_x[:, c, k:k + SEQ]
                        if k == 0:
                            ins = v.tensor_scalar(work[:, c, :], src, tap, None, ALU.mult)
                        else:
                            ins = v.scalar_tensor_tensor(out=work[:, c, :], in0=src, scalar=tap, in1=work[:, c, :],
                                                         op0=ALU.mult, op1=ALU.add)
                        ins.then_inc(conv_step, 1)
                dve.wait_ge(conv_step, PER * a + PER)
                dve.wait_ge(chunk_done, N_FIRST + 3 + 3 * a)
                v.tensor_tensor(area_d[:, bass.ds(CT * a, CT), :], work, channel_psum(N_FIRST + 2),
                                ALU.mult).then_inc(drained[0], 1)

            for c in range(N_OUT):
                n = N_IN + c
                dve.wait_ge(chunk_done, n + 1)
                for t in range(TT):
                    cols = slice(c * CW, (c + 1) * CW)
                    ins = v.scalar_tensor_tensor(out=area_a[:, t, cols], in0=area_b[:, t, cols], scalar=ALPHA,
                                                 in1=chunk_psum(n)[:, t, :], op0=ALU.mult, op1=ALU.add)
                    if t < TT - 1:
                        link(ins)
                ins.then_inc(drained[n % 3], 1)
                dve.wait_ge(drained[n % 3], n // 3 + 1)
                for t in range(TT):
                    link(v.bn_stats(stats[:, t, c, :], area_a[:, t, cols]))
            for t in range(TT):
                link(v.bn_aggr(mv[:, t, :], stats[:, t]))
            inverse_root(4)
            for t in range(TT):
                apply_norm(t, area_a[:, t, :], x1_ready, 2)

            def tile(n):
                return rt[:, n, :]

            def t2(ap, w=E):
                return ap.rearrange("p (t e) -> p t e", t=TT)

            probs, sel, val, pick1, pick2, picks, tmp, small = (tile(n) for n in range(8))
            dve.wait_ge(probs_ready, 1)
            link(v.tensor_tensor(t2(sel), t2(probs), b_rt[:].unsqueeze(1).to_broadcast([P, TT, E]), ALU.add))
            s4 = sel.rearrange("p (g e) -> p g e", e=GE)
            q = tmp.rearrange("p (n g) -> p n g", n=4)
            r = small.rearrange("p (n g) -> p n g", n=4)
            link(v.tensor_tensor(q[:, 0, :], s4[:, :, 0], s4[:, :, 1], ALU.max))
            link(v.tensor_tensor(q[:, 1, :], s4[:, :, 2], s4[:, :, 3], ALU.max))
            link(v.tensor_tensor(q[:, 2, :], s4[:, :, 0], s4[:, :, 1], ALU.min))
            link(v.tensor_tensor(q[:, 3, :], s4[:, :, 2], s4[:, :, 3], ALU.min))
            link(v.tensor_tensor(r[:, 0, :], q[:, 0, :], q[:, 1, :], ALU.max))
            link(v.tensor_tensor(r[:, 1, :], q[:, 0, :], q[:, 1, :], ALU.min))
            link(v.tensor_tensor(r[:, 2, :], q[:, 2, :], q[:, 3, :], ALU.max))
            link(v.tensor_tensor(r[:, 3, :], r[:, 1, :], r[:, 2, :], ALU.max))
            link(v.tensor_tensor(q[:, 0, :], r[:, 0, :], r[:, 3, :], ALU.add))

            best = rstd[:, :, 0]

            def first_largest(dst, scores, key, width, scratch):
                s3 = scores.rearrange("p (t e) -> p t e", t=TT)
                d3 = dst.rearrange("p (t e) -> p t e", t=TT)
                c3 = scratch.rearrange("p (t e) -> p t e", t=TT)
                wide = [P, TT, width]
                link(v.tensor_reduce(best, s3, AX_X, ALU.max))
                link(v.tensor_tensor(c3, s3, best.unsqueeze(2).to_broadcast(wide), ALU.is_equal))
                link(v.tensor_tensor(c3, c3, key, ALU.mult))
                link(v.tensor_reduce(best, c3, AX_X, ALU.max))
                link(v.tensor_tensor(d3, c3, best.unsqueeze(2).to_broadcast(wide), ALU.is_equal))

            first_largest(q[:, 1, :], q[:, 0, :], group_key[:], NG, q[:, 2, :])
            link(v.tensor_scalar(q[:, 3, :], q[:, 1, :], FAR, -FAR, ALU.mult, ALU.add))
            v4 = val.rearrange("p (g e) -> p g e", e=GE)
            wide = [P, TT * NG, GE]
            link(v.tensor_tensor(v4, s4, q[:, 1, :].unsqueeze(2).to_broadcast(wide), ALU.mult))
            link(v.tensor_tensor(v4, v4, q[:, 3, :].unsqueeze(2).to_broadcast(wide), ALU.add))
            first_largest(pick1, val, expert_key[:], E, tmp)
            link(v.scalar_tensor_tensor(out=val, in0=pick1, scalar=-2 * FAR, in1=val, op0=ALU.mult, op1=ALU.add))
            first_largest(pick2, val, expert_key[:], E, tmp)
            v.tensor_tensor(picks, pick1, pick2, ALU.add).then_inc(picks_ready, 1)
            sums = rstd
            for i, pick in enumerate((pick1, pick2)):
                link(v.tensor_tensor(tmp, pick, probs, ALU.mult))
                link(v.tensor_reduce(sums[:, :, 1 + i], t2(tmp), AX_X, ALU.add))
            link(v.tensor_tensor(best, sums[:, :, 1], sums[:, :, 2], ALU.add))
            link(v.reciprocal(best, best))
            for i, pick in enumerate((pick1, pick2)):
                link(v.tensor_tensor(sums[:, :, 1 + i], sums[:, :, 1 + i], best, ALU.mult))
                link(v.tensor_tensor(t2(pick), t2(pick), sums[:, :, 1 + i].unsqueeze(2).to_broadcast([P, TT, E]),
                                     ALU.mult))
            for b in range(BLOCKS + 1):
                link(v.tensor_tensor(gate[:, :, b * E:(b + 1) * E], t2(pick1), t2(pick2), ALU.add))
            dve.wait_ge(ranks_ready, 1)
            link(v.scalar_tensor_tensor(out=tmp, in0=psum[:, 1, 0:TT * E], scalar=1.0, in1=picks,
                                        op0=ALU.add, op1=ALU.mult))
            for b in range(BLOCKS + 1):
                link(v.tensor_scalar(rank[:, :, b * E:(b + 1) * E], t2(tmp), -1.0 - CAP * b, None, ALU.add))
            link(v.tensor_reduce(best[:, 0:1], psum[:, 1, 2 * E:3 * E], AX_X, ALU.max))
            v.tensor_scalar(overflow[:], best[:, 0:1], float(CAP), None, ALU.is_gt).then_inc(flag_ready, 1)

            def place(it):
                now = rank[:, :, bass.ds(2 * it, 2)].unsqueeze(3).to_broadcast([P, TT, 2, CAP])
                v.tensor_tensor(one_hot[:], slot_no[:].rearrange("p (t i) s -> p t i s", t=TT), now,
                                ALU.is_equal).then_inc(onehot_ready, 1)

            def step(it):
                dve.wait_ge(onehot_ready, it + 1)
                now = gate[:, :, bass.ds(2 * it, 2)].unsqueeze(3).to_broadcast([P, TT, 2, CAP])
                v.tensor_tensor(one_hot_g[:], one_hot[:], now, ALU.mult).then_inc(gated_ready, 1)
                dve.wait_ge(gather_ready, 4 * it + 4)
                dve.wait_ge(gated_ready, it + 1)
                place(it + 1)
                dve.wait_ge(silu_ready, it + 1)
                dve.wait_ge(chunk_done, STEP_CHUNKS * it + N_MIX + 4)
                v.tensor_tensor(hidden, silu_h, psum[:, 1, :], ALU.mult).then_inc(hidden_ready, 1)
                for c in range(NC):
                    dve.wait_ge(comb_ready, 4 * it + c + 1)
                    cols = slice(c * CW, (c + 1) * CW)
                    v.tensor_tensor(area_a[:, 0, cols], area_a[:, 0, cols], psum[:, 6, :], ALU.add)
                    v.tensor_tensor(area_a[:, 1, cols], area_a[:, 1, cols], psum[:, 7, :],
                                    ALU.add).then_inc(comb_added, 1)

            place(0)
            dve.wait_ge(res_ready, TT)
            with dve.Fori(0, PAIRS) as it:
                step(it)
            dve.wait_ge(comb_added, NC * PAIRS)
            more = dve.value_load(overflow[0:1, 0:1], min_val=0, max_val=1)
            with dve.If(more > 0):
                with dve.Fori(PAIRS, BLOCKS * PAIRS) as it:
                    step(it)
                dve.wait_ge(comb_added, NC * PAIRS * BLOCKS)
            with dve.Else():
                dve.nop()

            for t in range(TT):
                for c in range(NC):
                    link(v.bn_stats(stats[:, t, c, :], area_a[:, t, c * CW:(c + 1) * CW]))
                link(v.bn_aggr(mv[:, t, :], stats[:, t]))
            inverse_root(5)
            for t in range(TT):
                apply_norm(t, area_a[:, t, :], y_out, 3)


_INS = ["x", "ln_in_g", "ln_in_b", "w_in", "conv_a", "gate_ws", "gate_bs", "ln_v_g", "ln_v_b", "conv_c",
        "conv_c_b", "ln_c_g", "ln_c_b", "w_out", "ln1_g", "ln1_b", "w_router", "b_router", "w1", "w3", "w2",
        "ln2_g", "ln2_b"]


def kernel(**inputs):
    import numpy as _np
    import concourse.bacc as _bacc
    from concourse import mybir as _mybir
    from concourse.bass_utils import run_bass_kernel_spmd as _run

    nc = _bacc.Bacc("TRN2", target_bir_lowering=False, num_devices=1)
    arrays, args = {}, []
    for name in _INS:
        a = _np.ascontiguousarray(inputs[name])
        arrays[f"in_{name}_dram"] = a
        args.append(nc.dram_tensor(f"in_{name}_dram", a.shape, _mybir.dt.from_np(a.dtype), kind="ExternalInput").ap())
    shape = inputs["x"].shape
    args.append(nc.dram_tensor("out_0_dram", shape, _mybir.dt.float32, kind="ExternalOutput").ap())
    hybrid_layer(nc, *args)
    r = _run(nc, [arrays], core_ids=[0])
    return r.results[0]["out_0_dram"]
```

```python
from contextlib import ExitStack

import concourse.bass as bass
from concourse import mybir

P = 128
F32 = mybir.dt.float32
F32R = mybir.dt.float32r
I32 = mybir.dt.int32
ALU = mybir.AluOpType
ACT = mybir.ActivationFunctionType
AX_X = mybir.AxisListType.X
EPS = 1e-5
ALPHA = 2.0 ** 0.25
FAR = 1e30


def hybrid_layer(nc, x, ln_in_g, ln_in_b, w_in, conv_a, gate_ws, gate_bs, ln_v_g, ln_v_b,
                 conv_c, conv_c_b, ln_c_g, ln_c_b, w_out, ln1_g, ln1_b, w_router, b_router,
                 w1, w3, w2, ln2_g, ln2_b, out):
    _, SEQ, D = x.shape
    TT = SEQ // P
    KT = D // P
    TAPS_A, D_A = conv_a.shape[1:]
    TAPS_C, D_C = conv_c.shape[1:]
    HEADS = gate_ws.shape[1]
    BLK = gate_ws.shape[2]
    D_B = ln_v_g.shape[1]
    E = w_router.shape[1]
    FE = w1.shape[3]
    FT = FE // P
    CW = 512
    CT = CW // P
    NG, GE = 8, 4
    CAP = 64
    BLOCKS = SEQ // CAP
    PAIRS = E // 2
    NC = D // CW
    N_IN = w_in.shape[2] // CW
    N_OUT = NC
    N_MIX = N_IN + N_OUT
    STEP_CHUNKS = 6
    RING = 3
    HALF = KT // 2
    ROW_A = TAPS_C + 3
    ROWS = ROW_A + 2 * TAPS_A
    PAD_A, PAD_C = TAPS_A - 1, TAPS_C - 1
    assert TT == 2 and BLK == P and D_A == 2 * CW and D_B == D_C == CW and HEADS == CT
    assert STEP_CHUNKS % RING == 0
    UNIT = 4
    UNITS = KT // UNIT
    U_LEN = UNIT * CW
    N_UNITS = N_MIX * UNITS
    SPLITS = 3
    PRODUCTS = ((0, 0), (0, 1), (1, 0))

    def pool_lows(u):
        return u - u // UNITS

    B0, C0, XA0 = 0, D_A, 2 * D_A
    U0 = 3 * D_A
    V0, CA0, CG0 = U0 + D_B, U0 + 2 * D_B, U0 + 2 * D_B + D_C
    in_cols = [CA0, CG0, V0, U0] + [c + h * CW for h in range(2) for c in (C0, XA0, B0)]
    N_FIRST = 4
    assert len(in_cols) == N_IN

    with ExitStack() as ctx:
        def sb(name, shape, dt=F32):
            return ctx.enter_context(nc.sbuf_tensor(name, shape, dt))

        def sem(name):
            return ctx.enter_context(nc.semaphore(name))

        def aligned():
            return (nc.sbuf_base + 31) // 32 * 32

        ring_at = aligned()
        ring = sb("ring", [P, RING, 2, HALF * CW])
        area_a = sb("area_a", [P, TT, D])
        area_b = sb("area_b", [P, TT, D])
        c_at = aligned()
        area_c = sb("area_c", [P, KT, SEQ])
        area_d = sb("area_d", [P, KT, SEQ])
        area_g = sb("area_g", [P, 2, D])
        psum = ctx.enter_context(nc.psum_tensor("psum", [P, 8, CW], F32))

        chunk_bytes = 4 * 2 * HALF * CW
        raw = ring[:, 0]
        w_part = [[nc.alloc_sbuf_tensor_at(f"w_{name}{b}", [P, UNIT, CW], F32R,
                                           offset=ring_at + chunk_bytes + 4 * U_LEN * (2 * b + i))
                   for i, name in enumerate(("high", "low"))] for b in range(SPLITS)]
        in_part = [nc.alloc_sbuf_tensor_at("in_high", [P, KT, SEQ], F32R, offset=c_at),
                   nc.alloc_sbuf_tensor_at("in_low", [P, KT, SEQ], F32R,
                                           offset=ring_at + chunk_bytes + 4 * U_LEN * 2 * SPLITS)]
        assert 4 * (U_LEN * 2 * SPLITS + KT * SEQ) <= 2 * chunk_bytes

        def raw_unit(u):
            return raw[:, u // 2 % 2, (u % 2) * U_LEN:(u % 2 + 1) * U_LEN].rearrange("p (k c) -> p k c", k=UNIT)

        flat_a = area_a[:].rearrange("p t d -> p (t d)")
        flat_g = area_g[:].rearrange("p t d -> p (t d)")

        def quarter(flat, n):
            return flat[:, n * CT * SEQ:(n + 1) * CT * SEQ]

        plain = quarter(flat_a, 0).rearrange("p (c s) -> p c s", c=CT)
        sigm = quarter(flat_a, 1).rearrange("p (c s) -> p c s", c=CT)
        work = quarter(flat_a, 2).rearrange("p (c s) -> p c s", c=CT)
        v_rows = quarter(flat_a, 3).rearrange("p (k c) -> p k c", k=2)
        u_cm = quarter(flat_g, 0).rearrange("p (c s) -> p c s", c=CT)
        v_tm = quarter(flat_g, 1).rearrange("p (t c) -> p t c", t=TT)
        yc = quarter(flat_g, 2).rearrange("p (c s) -> p c s", c=CT)
        gate_shift = quarter(flat_g, 3)[:, 0:HEADS * BLK].rearrange("p (h i) -> p h i", h=HEADS)

        glu = sb("glu", [P, CT, PAD_C + SEQ])
        gated_x = sb("gated_x", [P, CT, PAD_A + SEQ])
        rows = sb("rows", [ROWS, CW])
        chan = sb("chan", [P, CT, ROWS])
        ws_raw = sb("ws_raw", [P, HEADS, BLK])
        ws_t = sb("ws_t", [P, HEADS, BLK])
        ident = sb("ident", [P, P])
        ones = sb("ones", [P, P])
        mean_w = sb("mean_w", [P, P])
        before = sb("before", [P, P])
        slot_no = sb("slot_no", [P, 2 * TT, CAP])
        group_key = sb("group_key", [P, TT, NG])
        expert_key = sb("expert_key", [P, TT, E])
        w_rt = sb("w_rt", [P, KT, E])
        b_rt = sb("b_rt", [P, E])
        stats = sb("stats", [P, TT, NC, 6])
        mv = sb("mv", [P, TT, 2])
        rstd = sb("rstd", [P, TT, 4])
        v_stats = sb("v_stats", [P, TT, 6])
        c_rstd = sb("c_rstd", [P, 2, SEQ])
        rank = sb("rank", [P, TT, (BLOCKS + 1) * E])
        gate = sb("gate", [P, TT, (BLOCKS + 1) * E])
        one_hot = sb("one_hot", [P, TT, 2, CAP])
        one_hot_g = sb("one_hot_g", [P, TT, 2, CAP])
        one_hot_gt = sb("one_hot_gt", [P, TT, P])
        overflow = sb("overflow", [P, 1], I32)

        flat_d = area_d[:].rearrange("p k s -> p (k s)")
        y_sb = flat_d[:, 0:D]
        silu_h = flat_d[:, D:D + CW]
        hidden = flat_d[:, D + CW:D + 2 * CW]
        hidden_t = flat_d[:, D + 2 * CW:D + 3 * CW].rearrange("p (f s) -> p f s", f=FT)
        rt = flat_d[:, D + 3 * CW:D + 4 * CW].rearrange("p (n w) -> p n w", w=TT * E)
        gathered = area_c[:].rearrange("p k s -> p (k s)")[:, 0:KT * P].rearrange("p (k s) -> p k s", k=KT)

        s_x = [sem(f"x_loaded{t}") for t in range(TT)]
        s_small, s_ws, s_g, s_vrow, s_out = (
            sem(n) for n in ("rows_loaded", "ws_loaded", "ln_rows_loaded", "v_rows_loaded", "stored"))
        raw_loaded = [sem(f"raw_half_loaded{i}") for i in range(2)]
        loaded = [sem(f"expert_chunk_loaded{i}") for i in range(RING)]
        high_ready, pool_low, dve_low = sem("high_ready"), sem("pool_low_ready"), sem("dve_low_ready")
        in_high, in_low = sem("in_high_ready"), sem("in_low_ready")
        consts = sem("consts_ready")
        units_done = sem("units_done")
        slots_free = sem("slots_free")
        drained = [sem(f"psum_drained{i}") for i in range(3)]
        extra_ready, extra_drained = sem("extra_ready"), sem("extra_drained")
        dve_step = sem("dve_step")
        var_ready, root_ready = sem("var_ready"), sem("root_ready")
        scale_ready, normed, stats_done = sem("norm_scale_ready"), sem("normed"), sem("stats_done")
        h0_ready, vn_ready, conv_c_step = sem("h0_ready"), sem("vn_ready"), sem("conv_c_step")
        z_ready, z_used, y_b_done = sem("z_ready"), sem("z_used"), sem("y_b_done")
        c_mean, c_sq, c_var, c_varused, c_norm, yc_done = (
            sem(n) for n in ("c_mean_ready", "c_squares_ready", "c_var_ready", "c_var_used", "c_normed", "y_c_done"))
        conv_step = sem("conv_a_step")
        x1_ready, res_ready = sem("x1_ready"), sem("residual_ready")
        logits_ready, probs_ready, picks_ready, ranks_ready = (
            sem(n) for n in ("logits_ready", "probs_ready", "picks_ready", "ranks_ready"))
        flag_ready = sem("flag_ready")
        onehot_ready, gated_ready = sem("onehot_ready"), sem("gated_onehot_ready")
        gather_ready, gather_drained = sem("gather_ready"), sem("gather_drained")
        silu_ready, hidden_ready = sem("silu_ready"), sem("hidden_ready")
        ht_ready, ht_drained = sem("hidden_t_ready"), sem("hidden_t_drained")
        gt_ready, gt_drained = sem("onehot_t_ready"), sem("onehot_t_drained")
        y_ready, y_drained = sem("y_ready"), sem("y_drained")
        comb_ready, comb_added = sem("combined_ready"), sem("combined_added")
        y_out = sem("y_out")

        def chunk_psum(n):
            b = 2 * (n % 3)
            return psum[:, b:b + 2, :]

        def channel_psum(n):
            return chunk_psum(n).rearrange("p b (c s) -> p (b c) s", s=SEQ)

        def spread(row):
            return row.partition_broadcast(P)

        block = ctx.enter_context(nc.Block())

        @block.sync
        def _(sp):
            for t in range(TT):
                sp.dma_start(area_a[:, t, :], x[0, t * P:(t + 1) * P, :]).then_inc(s_x[t], 16)

            sp.dma_start(area_g[:, 0, :], spread(ln_in_g)).then_inc(s_g, 16)
            sp.dma_start(area_g[:, 1, :], spread(ln_in_b)).then_inc(s_g, 16)
            for m in range(2 * N_MIX):
                n, h = divmod(m, 2)
                if n < N_IN:
                    src = w_in[0][:, in_cols[n]:in_cols[n] + CW]
                else:
                    src = w_out[0][:, (n - N_IN) * CW:(n - N_IN + 1) * CW]
                if m >= 2:
                    sp.wait_ge(pool_low, pool_lows(2 * m - 2))
                    if m >= 3:
                        sp.wait_ge(dve_low, (2 * m - 2) // UNITS)
                sp.dma_start(raw[:, h].rearrange("p (k c) -> p k c", k=HALF),
                             src.rearrange("(h k p) c -> h p k c", h=2, p=P)[h]).then_inc(raw_loaded[h], 16)
            sp.wait_ge(units_done, UNITS * (N_IN + 1))
            sp.dma_start(area_g[:, 0, :], spread(ln1_g[0])).then_inc(s_g, 16)
            sp.dma_start(area_g[:, 1, :], spread(ln1_b[0])).then_inc(s_g, 16)
            sp.wait_ge(units_done, N_UNITS)
            sp.sem_inc(slots_free, RING)

            def load_step(it, pair):
                for j in range(STEP_CHUNKS):
                    slot = j % RING
                    sp.wait_ge(slots_free, STEP_CHUNKS * it + j + 1)
                    for i in range(2):
                        e = 2 * pair + i
                        if j < 4:
                            src = (w1, w3)[j // 2][0, e].rearrange("(h k p) f -> h p k f", h=2, p=P)[j % 2]
                            dst = ring[:, slot, i, :].rearrange("p (k f) -> p k f", k=HALF)
                        else:
                            src = w2[0, e].rearrange("(f p) (h d) -> h p f d", p=P, h=2)[j % 2]
                            dst = ring[:, slot, i, :].rearrange("p (f d) -> p f d", f=FT)
                        sp.dma_start(dst, src).then_inc(loaded[slot], 16)

            with sp.Fori(0, PAIRS) as it:
                load_step(it, it)
            sp.wait_ge(x1_ready, 2 * TT)
            sp.dma_start(area_g[:, 0, :], spread(ln2_g[0])).then_inc(s_g, 16)
            sp.dma_start(area_g[:, 1, :], spread(ln2_b[0])).then_inc(s_g, 16)
            sp.wait_ge(flag_ready, 1)
            more = sp.value_load(overflow[0:1, 0:1], min_val=0, max_val=1)
            with sp.If(more > 0):
                with sp.Fori(1, BLOCKS) as b:
                    with sp.Fori(0, PAIRS) as p:
                        load_step(b * PAIRS + p, p)
                sp.nop()
            with sp.Else():
                sp.nop()
            for t in range(TT):
                for h in range(2):
                    sp.wait_ge(y_out, 2 * t + h + 1)
                    cols = slice(h * D // 2, (h + 1) * D // 2)
                    sp.dma_start(out[0, t * P:(t + 1) * P, cols], area_b[:, t, cols]).then_inc(s_out, 16)
            sp.wait_ge(s_out, 16 * 2 * TT)

        @block.gpsimd
        def _(pool):
            nc.gpsimd.memset(ones[:], 1.0).then_inc(consts, 1)
            nc.gpsimd.memset(mean_w[:], 1.0 / D_C).then_inc(consts, 1)
            pool.wait_ge(consts, 1)
            nc.gpsimd.affine_select(out=ident[:], in_=ones[:], compare_op=ALU.is_equal, fill=0.0, base=0,
                                    pattern=[[-1, P]], channel_multiplier=1).then_inc(consts, 1)
            nc.gpsimd.affine_select(out=before[:], in_=ones[:], compare_op=ALU.is_gt, fill=0.0, base=0,
                                    pattern=[[1, P]], channel_multiplier=-1).then_inc(consts, 1)
            nc.gpsimd.iota(slot_no[:], pattern=[[0, 2 * TT], [1, CAP]], base=0, channel_multiplier=0,
                           allow_small_or_imprecise_dtypes=True).then_inc(consts, 1)
            nc.gpsimd.iota(group_key[:], pattern=[[0, TT], [-1, NG]], base=NG, channel_multiplier=0,
                           allow_small_or_imprecise_dtypes=True).then_inc(consts, 1)
            nc.gpsimd.iota(expert_key[:], pattern=[[0, TT], [-1, E]], base=E, channel_multiplier=0,
                           allow_small_or_imprecise_dtypes=True).then_inc(consts, 1)
            nc.gpsimd.memset(glu[:, :, 0:PAD_C], 0.0).then_inc(consts, 1)
            nc.gpsimd.memset(gated_x[:, :, 0:PAD_A], 0.0).then_inc(consts, 1)
            pool.wait_ge(consts, 9)
            nc.gpsimd.memset(ws_t[P // 2:P, :, 0:BLK // 2], 0.0).then_inc(consts, 1)
            for u in range(N_UNITS):
                if u % UNITS < UNITS - 1:
                    pool.wait_ge(high_ready, u + 1)
                    high, low = w_part[u % SPLITS]
                    nc.gpsimd.tensor_tensor(low[:], raw_unit(u), high[:].bitcast(F32),
                                            ALU.subtract).then_inc(pool_low, 1)
        CONSTS = 10

        @block.tensor
        def _(pe):
            pe.wait_ge(consts, CONSTS)
            pe.wait_ge(s_small, 16 * 6)
            for c in range(CT):
                mm = pe.transpose(psum[:, 6, c * ROWS:(c + 1) * ROWS], rows[:, c * P:(c + 1) * P],
                                  ident[0:ROWS, 0:ROWS])
            mm.then_inc(extra_ready, 1)
            pe.wait_ge(s_ws, 16)
            for h in range(HEADS):
                mm = pe.transpose(psum[:, 7, h * P:(h + 1) * P], ws_raw[:, h, :], ident[:])
            mm.then_inc(extra_ready, 1)

            def turn_rows(ready, t):
                for g in range(KT // 4):
                    if g % 2 == 0:
                        pe.wait_ge(ready, 2 * t + g // 2 + 1)
                    for j in range(4):
                        k = 4 * g + j
                        mm = pe.transpose(psum[:, 4 * t + g, j * P:(j + 1) * P],
                                          area_b[:, t, k * P:(k + 1) * P], ident[:])
                    mm.then_inc(extra_ready, 1)

            turn_rows(h0_ready, 0)
            pe.wait_ge(extra_drained, 2)
            turn_rows(h0_ready, 1)
            pe.wait_ge(in_high, TT * KT // 4)
            pe.wait_ge(in_low, TT * KT // 4)

            def unit(u):
                pe.wait_ge(high_ready, u + 1)
                if u % UNITS < UNITS - 1:
                    pe.wait_ge(pool_low, pool_lows(u + 1))
                else:
                    pe.wait_ge(dve_low, u // UNITS + 1)
                return w_part[u % SPLITS]

            def channels(n):
                if n >= 3:
                    pe.wait_ge(drained[n % 3], n // 3)
                o = channel_psum(n)
                for q in range(UNITS):
                    w = unit(UNITS * n + q)
                    for k in range(UNIT):
                        kk = UNIT * q + k
                        for c in range(CT):
                            for a, b in PRODUCTS:
                                mm = pe.matmul(o[:, c, :], w[a][:, k, c * P:(c + 1) * P], in_part[b][:, kk, :],
                                               start=kk == 0 and a + b == 0 and c % 2 == 0,
                                               stop=kk == KT - 1 and a == 1, skip_group_check=True)
                    mm.then_inc(units_done, 1)

            def tokens(n):
                if n >= 3:
                    pe.wait_ge(drained[n % 3], n // 3)
                o = chunk_psum(n)
                for q in range(UNITS):
                    w = unit(UNITS * n + q)
                    if n == N_IN:
                        pe.wait_ge(in_high, TT * KT // 4 + q + 1)
                        pe.wait_ge(in_low, TT * KT // 4 + q + 1)
                    for k in range(UNIT):
                        kk = UNIT * q + k
                        for t in range(TT):
                            for a, b in PRODUCTS:
                                mm = pe.matmul(o[:, t, :], in_part[a][:, kk, t * P:(t + 1) * P], w[b][:, k, :],
                                               start=kk == 0 and a + b == 0, stop=kk == KT - 1 and a == 1)
                    mm.then_inc(units_done, 1)

            channels(0)
            channels(1)
            tokens(2)
            channels(3)
            channels(4)
            pe.wait_ge(vn_ready, 1)
            z = psum[:, 6:8, :].rearrange("p b (h s) -> p (b h) s", s=SEQ)
            for h in range(HEADS):
                for t in range(TT):
                    mm = pe.matmul(z[:, h, t * P:(t + 1) * P], v_tm[:, t, h * P:(h + 1) * P], ws_t[:, h, :],
                                   start=True, stop=True)
            mm.then_inc(z_ready, 1)
            channels(5)
            pe.wait_ge(z_used, 1)
            pe.wait_ge(conv_c_step, TAPS_C * CT)
            for c in range(CT):
                mm = pe.matmul(psum[:, 6, 0:SEQ], mean_w[:], yc[:, c, :], start=c == 0, stop=c == CT - 1)
            mm.then_inc(c_mean, 1)
            channels(6)
            channels(7)
            pe.wait_ge(c_sq, 1)
            for c in range(CT):
                mm = pe.matmul(psum[:, 7, 0:SEQ], mean_w[:], sigm[:, c, :], start=c == 0, stop=c == CT - 1)
            mm.then_inc(c_var, 1)
            channels(8)
            channels(9)
            for c in range(N_OUT):
                tokens(N_IN + c)

            for b in range(3):
                pe.wait_ge(drained[b], -(-(N_MIX - b) // 3))
            pe.wait_ge(c_varused, 1)
            for t in range(TT):
                turn_rows(x1_ready, t)
            pe.wait_ge(extra_drained, 2 + TT * KT // 4)
            for t in range(TT):
                for k in range(KT):
                    mm = pe.matmul(psum[:, 0, t * E:(t + 1) * E], area_c[:, k, t * P:(t + 1) * P],
                                   w_rt[:, k, :], start=k == 0, stop=k == KT - 1)
            mm.then_inc(logits_ready, 1)
            pe.wait_ge(picks_ready, 1)
            picks = rt[:, 5, :].rearrange("p (t e) -> p t e", t=TT)
            pe.matmul(psum[:, 1, 0:E], before[:], picks[:, 0, :], start=True, stop=True)
            pe.matmul(psum[:, 1, E:2 * E], ones[:], picks[:, 0, :], start=True, stop=False)
            pe.matmul(psum[:, 1, E:2 * E], before[:], picks[:, 1, :], start=False, stop=True)
            pe.matmul(psum[:, 1, 2 * E:3 * E], ones[:], picks[:, 0, :], start=True, stop=False)
            pe.matmul(psum[:, 1, 2 * E:3 * E], ones[:], picks[:, 1, :], start=False, stop=True).then_inc(ranks_ready, 1)

            def gather(it):
                pe.wait_ge(onehot_ready, it + 1)
                for g in range(KT // 4):
                    if g >= 2:
                        pe.wait_ge(gather_drained, 4 * it + g - 1)
                    for j in range(4):
                        k = 4 * g + j
                        for t in range(TT):
                            mm = pe.matmul(psum[:, 2 + g % 2, j * P:(j + 1) * P],
                                           area_b[:, t, k * P:(k + 1) * P],
                                           one_hot[:, t].rearrange("p i s -> p (i s)"),
                                           start=t == 0, stop=t == TT - 1)
                    mm.then_inc(gather_ready, 1)

            def step(it):
                pe.wait_ge(gather_drained, 4 * it + 4)
                for j in range(4):
                    slot = j % RING
                    pe.wait_ge(loaded[slot], 64 * it + 32 * (j // RING + 1))
                    bank = j // 2
                    for k in range(HALF):
                        kk = (j % 2) * HALF + k
                        for i in range(2):
                            mm = pe.matmul(psum[i * CAP:(i + 1) * CAP, bank, :],
                                           gathered[:, kk, i * CAP:(i + 1) * CAP],
                                           ring[:, slot, i, k * CW:(k + 1) * CW],
                                           start=kk == 0, stop=kk == KT - 1)
                    mm.then_inc(slots_free, 1)
                gather(it + 1)
                pe.wait_ge(hidden_ready, it + 1)
                pe.wait_ge(gather_drained, 4 * it + 7)
                for f in range(FT):
                    mm = pe.transpose(psum[:, 2, f * P:(f + 1) * P], hidden[:, f * P:(f + 1) * P], ident[:])
                mm.then_inc(ht_ready, 1)
                pe.wait_ge(gated_ready, it + 1)
                pe.wait_ge(gather_drained, 4 * it + 8)
                for t in range(TT):
                    mm = pe.transpose(psum[:, 3, t * P:(t + 1) * P],
                                      one_hot_g[:, t].rearrange("p i s -> p (i s)"), ident[:])
                mm.then_inc(gt_ready, 1)
                pe.wait_ge(ht_drained, it + 1)

                def project(c):
                    j = 4 + c // 2
                    slot = j % RING
                    if c % 2 == 0:
                        pe.wait_ge(loaded[slot], 64 * it + 32 * (j // RING + 1))
                    if c >= 2:
                        pe.wait_ge(y_drained, 4 * it + c - 1)
                    for f in range(FT):
                        for i in range(2):
                            at = f * (D // 2) + (c % 2) * CW
                            mm = pe.matmul(psum[i * CAP:(i + 1) * CAP, 4 + c % 2, :],
                                           hidden_t[:, f, i * CAP:(i + 1) * CAP],
                                           ring[:, slot, i, at:at + CW], start=f == 0, stop=f == FT - 1)
                    mm.then_inc(y_ready, 1)

                def combine(c):
                    pe.wait_ge(y_drained, 4 * it + c + 1)
                    if c == 0:
                        pe.wait_ge(gt_drained, it + 1)
                    else:
                        pe.wait_ge(comb_added, 4 * it + c)
                    for t in range(TT):
                        mm = pe.matmul(psum[:, 6 + t, :], one_hot_gt[:, t, :], y_sb[:, c * CW:(c + 1) * CW],
                                       start=True, stop=True)
                        if t == 0 and c % 2 == 0:
                            mm.then_inc(slots_free, 1)
                    mm.then_inc(comb_ready, 1)

                project(0)
                project(1)
                combine(0)
                project(2)
                combine(1)
                project(3)
                combine(2)
                combine(3)

            gather(0)
            with pe.Fori(0, PAIRS) as it:
                step(it)
            pe.wait_ge(flag_ready, 1)
            more = pe.value_load(overflow[0:1, 0:1], min_val=0, max_val=1)
            with pe.If(more > 0):
                with pe.Fori(PAIRS, BLOCKS * PAIRS) as it:
                    step(it)
                pe.nop()
            with pe.Else():
                pe.nop()

        @block.scalar
        def _(act):
            act.dma_start(rows[0:TAPS_C, :], conv_c[0]).then_inc(s_small, 16)
            for r, src in enumerate((conv_c_b, ln_c_g, ln_c_b)):
                act.dma_start(rows[TAPS_C + r:TAPS_C + r + 1, :], src).then_inc(s_small, 16)
            for h in range(2):
                act.dma_start(rows[ROW_A + h * TAPS_A:ROW_A + (h + 1) * TAPS_A, :],
                              conv_a[0][:, h * CW:(h + 1) * CW]).then_inc(s_small, 16)
            act.dma_start(ws_raw[:], gate_ws[0].rearrange("h i j -> i h j")).then_inc(s_ws, 16)
            act.dma_start(w_rt[:], w_router.rearrange("(k p) e -> p k e", p=P)).then_inc(s_vrow, 16)
            act.dma_start(b_rt[:], spread(b_router)).then_inc(s_vrow, 16)

            act.wait_ge(extra_ready, 1)
            act.activation(chan[:], psum[:, 6, 0:CT * ROWS].rearrange("p (c r) -> p c r", c=CT),
                           ACT.Copy).then_inc(extra_drained, 1)
            act.wait_ge(extra_ready, 2)
            wsp = psum[:, 7, :].rearrange("p (h i) -> p h i", h=HEADS)
            act.activation(ws_t[0:P // 2], wsp[0:P // 2], ACT.Copy)
            act.activation(ws_t[P // 2:P, :, BLK // 2:], wsp[P // 2:P, :, BLK // 2:],
                           ACT.Copy).then_inc(extra_drained, 1)

            def root(n, t):
                act.wait_ge(var_ready, n)
                act.activation(rstd[:, t, 1], rstd[:, t, 0], ACT.Sqrt).then_inc(root_ready, 1)

            def normalise(n):
                for t in range(TT):
                    act.wait_ge(scale_ready, TT * n + t + 1)
                    for h in range(2):
                        cols = slice(h * D // 2, (h + 1) * D // 2)
                        act.activation(area_b[:, t, cols], area_a[:, t, cols], ACT.Identity,
                                       scale=rstd[:, t, 2:3], bias=rstd[:, t, 3:4]).then_inc(normed, 1)

            def high(u):
                act.wait_ge(raw_loaded[u // 2 % 2], 16 * (u // UNITS + 1))
                if u >= SPLITS:
                    act.wait_ge(units_done, u - SPLITS + 1)
                act.activation(w_part[u % SPLITS][0][:], raw_unit(u), ACT.Copy).then_inc(high_ready, 1)

            for t in range(TT):
                root(1 + t, slice(t, t + 1))
            normalise(0)
            for g in range(TT * KT // 4):
                t, k = divmod(4 * g, KT)
                act.wait_ge(extra_ready, 2 + g + 1)
                act.activation(in_part[0][:, k:k + 4, t * P:(t + 1) * P],
                               psum[:, g, :].rearrange("p (j s) -> p j s", j=4), ACT.Copy).then_inc(in_high, 1)
            act.wait_ge(h0_ready, 2 * TT)
            act.dma_start(v_rows[:, 0, :], spread(ln_v_g[0])).then_inc(s_vrow, 16)
            act.dma_start(v_rows[:, 1, :], spread(ln_v_b[0])).then_inc(s_vrow, 16)
            act.dma_start(gate_shift, spread(gate_bs[0])).then_inc(s_vrow, 16)

            def after_chunk(n):
                act.wait_ge(units_done, UNITS * (n + 1))
                if n == 0:
                    act.activation(plain, channel_psum(n), ACT.Copy).then_inc(drained[0], 1)
                elif n == 1:
                    act.activation(sigm, channel_psum(n), ACT.Sigmoid).then_inc(drained[1], 1)
                elif n == 3:
                    act.activation(u_cm, channel_psum(n), ACT.Copy).then_inc(drained[0], 1)
                elif n == 4 or n == 7:
                    if n == 4:
                        act.wait_ge(conv_c_step, CT)
                    else:
                        act.wait_ge(drained[2], 2)
                    act.activation(plain, channel_psum(n), ACT.Copy).then_inc(drained[1], 1)
                elif n == 8:
                    act.wait_ge(c_norm, 1)
                    for c in range(CT):
                        act.activation(area_d[:, 12 + c, :], yc[:, c, :], ACT.Silu,
                                       scale=chan[:, c, TAPS_C + 1:TAPS_C + 2],
                                       bias=chan[:, c, TAPS_C + 2:TAPS_C + 3]).then_inc(yc_done, 1)
                elif n == N_IN - 1:
                    for q in range(UNITS):
                        if q == 1:
                            act.wait_ge(drained[0], 4)
                        elif q == 2:
                            act.wait_ge(y_b_done, 1)
                        rows_q = slice(4 * q, 4 * q + 4)
                        act.activation(in_part[0][:, rows_q, :], area_d[:, rows_q, :],
                                       ACT.Copy).then_inc(in_high, 1)

            for u in range(N_UNITS):
                high(u)
                if u == 4 * UNITS + 1:
                    root(3, slice(0, TT))
                if u == 9 * UNITS - 1:
                    act.wait_ge(c_varused, 1)
                    act.activation(c_rstd[:, 1, :], c_rstd[:, 0, :], ACT.Sqrt).then_inc(root_ready, 1)
                n, q = divmod(u - 1, UNITS)
                if q == 0 and 1 <= n <= N_IN:
                    after_chunk(n - 1)

            for t in range(TT):
                root(4 + t, slice(t, t + 1))
            normalise(1)
            for g in range(TT * KT // 4):
                t, k = divmod(4 * g, KT)
                act.wait_ge(extra_ready, 2 + TT * KT // 4 + g + 1)
                act.activation(area_c[:, k:k + 4, t * P:(t + 1) * P],
                               psum[:, g, :].rearrange("p (j s) -> p j s", j=4), ACT.Copy).then_inc(extra_drained, 1)
            act.wait_ge(logits_ready, 1)
            act.activation(rt[:, 0, :], psum[:, 0, 0:TT * E], ACT.Sigmoid).then_inc(probs_ready, 1)
            for t in range(TT):
                act.activation(area_a[:, t, :], area_b[:, t, :], ACT.Copy, scale=ALPHA).then_inc(res_ready, 1)

            def keep_gathered(it):
                for g in range(KT // 4):
                    act.wait_ge(gather_ready, 4 * it + g + 1)
                    act.activation(gathered[:, 4 * g:4 * g + 4, :],
                                   psum[:, 2 + g % 2, :].rearrange("p (j s) -> p j s", j=4),
                                   ACT.Copy).then_inc(gather_drained, 1)

            def step(it):
                act.wait_ge(slots_free, STEP_CHUNKS * it + RING + 2)
                act.activation(silu_h, psum[:, 0, :], ACT.Silu).then_inc(silu_ready, 1)
                keep_gathered(it + 1)
                act.wait_ge(ht_ready, it + 1)
                act.activation(hidden_t, psum[:, 2, :].rearrange("p (f s) -> p f s", f=FT),
                               ACT.Copy).then_inc(ht_drained, 1)
                act.wait_ge(gt_ready, it + 1)
                act.activation(one_hot_gt[:], psum[:, 3, 0:TT * P].rearrange("p (t s) -> p t s", t=TT),
                               ACT.Copy).then_inc(gt_drained, 1)
                for c in range(NC):
                    act.wait_ge(y_ready, 4 * it + c + 1)
                    act.activation(y_sb[:, c * CW:(c + 1) * CW], psum[:, 4 + c % 2, :],
                                   ACT.Copy).then_inc(y_drained, 1)

            keep_gathered(0)
            with act.Fori(0, PAIRS) as it:
                step(it)
            act.wait_ge(flag_ready, 1)
            more = act.value_load(overflow[0:1, 0:1], min_val=0, max_val=1)
            with act.If(more > 0):
                with act.Fori(PAIRS, BLOCKS * PAIRS) as it:
                    step(it)
                act.nop()
            with act.Else():
                act.nop()
            for t in range(TT):
                root(6 + t, slice(t, t + 1))
            normalise(2)

        @block.vector
        def _(dve):
            v = nc.vector
            steps = [0]

            def link(ins):
                steps[0] += 1
                ins.then_inc(dve_step, 1)
                dve.wait_ge(dve_step, steps[0])

            def variance(t):
                v.tensor_scalar(rstd[:, t, 0], mv[:, t, 1], EPS, None, ALU.add).then_inc(var_ready, 1)

            def inverse_root(n, t):
                dve.wait_ge(root_ready, n)
                link(v.reciprocal(rstd[:, t, 2], rstd[:, t, 1]))

            def norm_scale(n, t):
                one = slice(t, t + 1)
                inverse_root(n, one)
                v.scalar_tensor_tensor(out=rstd[:, one, 3], in0=mv[:, one, 0], scalar=-1.0, in1=rstd[:, one, 2],
                                       op0=ALU.mult, op1=ALU.mult).then_inc(scale_ready, 1)

            def scale_shift(n, ready):
                for t in range(TT):
                    for h in range(2):
                        cols = slice(h * D // 2, (h + 1) * D // 2)
                        dst = area_b[:, t, cols]
                        dve.wait_ge(normed, 2 * TT * n + 2 * t + h + 1)
                        if t == 0 and h == 0:
                            dve.wait_ge(s_g, 32 * (n + 1))
                        link(v.tensor_tensor(dst, dst, area_g[:, 0, cols], ALU.mult))
                        v.tensor_tensor(dst, dst, area_g[:, 1, cols], ALU.add).then_inc(ready, 1)

            for t in range(TT):
                dve.wait_ge(s_x[t], 16)
                for c in range(NC):
                    link(v.bn_stats(stats[:, t, c, :], area_a[:, t, c * CW:(c + 1) * CW]))
                link(v.bn_aggr(mv[:, t, :], stats[:, t]))
                variance(slice(t, t + 1))
            for t in range(TT):
                norm_scale(1 + t, t)
            scale_shift(0, h0_ready)

            for g in range(TT * KT // 4):
                t, k = divmod(4 * g, KT)
                dve.wait_ge(in_high, g + 1)
                at = slice(k, k + 4), slice(t * P, (t + 1) * P)
                v.tensor_tensor(in_part[1][:, at[0], at[1]], psum[:, g, :].rearrange("p (j s) -> p j s", j=4),
                                in_part[0][:, at[0], at[1]].bitcast(F32), ALU.subtract).then_inc(in_low, 1)

            def low(n):
                u = UNITS * n + UNITS - 1
                dve.wait_ge(high_ready, u + 1)
                high, rest = w_part[u % SPLITS]
                v.tensor_tensor(rest[:], raw_unit(u), high[:].bitcast(F32), ALU.subtract).then_inc(dve_low, 1)

            def glu_product():
                dve.wait_ge(drained[0], 1)
                dve.wait_ge(drained[1], 1)
                dve.wait_ge(consts, CONSTS)
                dve.wait_ge(extra_drained, 2)
                link(v.tensor_tensor(glu[:, :, PAD_C:], plain, sigm, ALU.mult))

            def conv_c_taps(first, end):
                for k in range(first, end):
                    for c in range(CT):
                        if k >= 1:
                            dve.wait_ge(conv_c_step, (k - 1) * CT + c + 1)
                        tap = chan[:, c, k:k + 1]
                        src = glu[:, c, k:k + SEQ]
                        if k == 0:
                            ins = v.tensor_scalar(yc[:, c, :], src, tap, chan[:, c, TAPS_C:TAPS_C + 1],
                                                  ALU.mult, ALU.add)
                        else:
                            ins = v.scalar_tensor_tensor(out=yc[:, c, :], in0=src, scalar=tap, in1=yc[:, c, :],
                                                         op0=ALU.mult, op1=ALU.add)
                        ins.then_inc(conv_c_step, 1)

            v_ps = chunk_psum(2)

            def v_statistics():
                dve.wait_ge(units_done, 3 * UNITS)
                for t in range(TT):
                    link(v.bn_stats(v_stats[:, t, :], v_ps[:, t, :]))
                    link(v.bn_aggr(mv[:, t, :], v_stats[:, t:t + 1, :]))
                variance(slice(0, TT))

            def v_normalise():
                inverse_root(3, slice(0, TT))
                link(v.tensor_scalar(v_tm[:, 0, :], v_ps[:, 0, :], mv[:, 0, 0:1], rstd[:, 0, 2:3],
                                     ALU.subtract, ALU.mult))
                v.tensor_scalar(v_tm[:, 1, :], v_ps[:, 1, :], mv[:, 1, 0:1], rstd[:, 1, 2:3],
                                ALU.subtract, ALU.mult).then_inc(drained[2], 1)
                dve.wait_ge(drained[2], 1)
                dve.wait_ge(s_vrow, 16 * 5)
                link(v.tensor_tensor(v_tm, v_tm, v_rows[:, 0:1, :].to_broadcast([P, TT, CW]), ALU.mult))
                v.tensor_tensor(v_tm, v_tm, v_rows[:, 1:2, :].to_broadcast([P, TT, CW]),
                                ALU.add).then_inc(vn_ready, 1)

            def gate_b():
                dve.wait_ge(z_ready, 1)
                z = psum[:, 6:8, :].rearrange("p b (h s) -> p (b h) s", s=SEQ)
                link(v.tensor_tensor(work[:, :, 0:P], z[:, :, 0:P], gate_shift, ALU.add))
                v.tensor_tensor(work[:, :, P:SEQ], z[:, :, P:SEQ], gate_shift, ALU.add).then_inc(z_used, 1)
                dve.wait_ge(z_used, 1)
                dve.wait_ge(drained[0], 2)
                v.tensor_tensor(area_d[:, 8:12, :], work, u_cm, ALU.mult).then_inc(y_b_done, 1)

            def norm_c_difference():
                dve.wait_ge(c_mean, 1)
                mean = psum[:, 6:7, 0:SEQ].to_broadcast([P, CT, SEQ])
                link(v.tensor_tensor(yc, yc, mean, ALU.subtract))
                v.tensor_tensor(sigm, yc, yc, ALU.mult).then_inc(c_sq, 1)

            def norm_c():
                dve.wait_ge(c_var, 1)
                v.tensor_scalar(c_rstd[:, 0, :], psum[:, 7, 0:SEQ], EPS, None, ALU.add).then_inc(c_varused, 1)
                dve.wait_ge(root_ready, 4)
                link(v.reciprocal(c_rstd[:, 0, :], c_rstd[:, 1, :]))
                v.tensor_tensor(yc, yc, c_rstd[:, 0:1, :].to_broadcast([P, CT, SEQ]), ALU.mult).then_inc(c_norm, 1)

            def conv_a_half(a):
                n = N_FIRST + 3 * a
                dve.wait_ge(units_done, UNITS * (n + 2))
                dve.wait_ge(drained[1], 2 + a)
                v.tensor_tensor(gated_x[:, :, PAD_A:], plain, channel_psum(n + 1), ALU.mult).then_inc(drained[2], 1)
                dve.wait_ge(drained[2], 2 + a)
                dve.wait_ge(y_b_done, 1)
                first = CT * TAPS_A * a
                for k in range(TAPS_A):
                    for c in range(CT):
                        if k >= 1:
                            dve.wait_ge(conv_step, first + (k - 1) * CT + c + 1)
                        tap = chan[:, c, ROW_A + TAPS_A * a + k:ROW_A + TAPS_A * a + k + 1]
                        src = gated_x[:, c, k:k + SEQ]
                        if k == 0:
                            ins = v.tensor_scalar(work[:, c, :], src, tap, None, ALU.mult)
                        else:
                            ins = v.scalar_tensor_tensor(out=work[:, c, :], in0=src, scalar=tap, in1=work[:, c, :],
                                                         op0=ALU.mult, op1=ALU.add)
                        ins.then_inc(conv_step, 1)
                dve.wait_ge(conv_step, first + CT * TAPS_A)

            def gate_a(a):
                n = N_FIRST + 3 * a + 2
                dve.wait_ge(units_done, UNITS * (n + 1))
                v.tensor_tensor(area_d[:, CT * a:CT * (a + 1), :], work, channel_psum(n),
                                ALU.mult).then_inc(drained[0], 1)

            def low_output(q):
                dve.wait_ge(in_high, TT * KT // 4 + q + 1)
                tiles = slice(4 * q, 4 * q + 4)
                v.tensor_tensor(in_part[1][:, tiles, :], area_d[:, tiles, :], in_part[0][:, tiles, :].bitcast(F32),
                                ALU.subtract).then_inc(in_low, 1)

            def residual(n):
                dve.wait_ge(units_done, UNITS * (n + 1))
                cols = slice((n - N_IN) * CW, (n - N_IN + 1) * CW)
                for t in range(TT):
                    ins = v.scalar_tensor_tensor(out=area_a[:, t, cols], in0=area_b[:, t, cols], scalar=ALPHA,
                                                 in1=chunk_psum(n)[:, t, :], op0=ALU.mult, op1=ALU.add)
                    if t < TT - 1:
                        link(ins)
                ins.then_inc(drained[n % 3], 1)
                dve.wait_ge(drained[n % 3], n // 3 + 1)
                for t in range(TT):
                    link(v.bn_stats(stats[:, t, n - N_IN, :], area_a[:, t, cols]))

            low(0)
            low(1)
            low(2)
            glu_product()
            conv_c_taps(0, 10)
            low(3)
            v_statistics()
            conv_c_taps(10, 16)
            low(4)
            v_normalise()
            conv_c_taps(16, 23)
            low(5)
            gate_b()
            conv_c_taps(23, TAPS_C)
            low(6)
            norm_c_difference()
            conv_a_half(0)
            low(7)
            gate_a(0)
            low(8)
            norm_c()
            low(9)
            conv_a_half(1)
            dve.wait_ge(units_done, UNITS * N_IN)
            low_output(0)
            gate_a(1)
            for q in range(1, UNITS):
                low_output(q)
            low(10)
            for n in range(N_IN, N_MIX):
                if n < N_MIX - 1:
                    low(n + 1)
                residual(n)

            for t in range(TT):
                link(v.bn_aggr(mv[:, t, :], stats[:, t]))
                variance(slice(t, t + 1))
            for t in range(TT):
                norm_scale(5 + t, t)
            scale_shift(1, x1_ready)

            def tile(n):
                return rt[:, n, :]

            def t2(ap, w=E):
                return ap.rearrange("p (t e) -> p t e", t=TT)

            probs, sel, val, pick1, pick2, picks, tmp, small = (tile(n) for n in range(8))
            dve.wait_ge(probs_ready, 1)
            link(v.tensor_tensor(t2(sel), t2(probs), b_rt[:].unsqueeze(1).to_broadcast([P, TT, E]), ALU.add))
            s4 = sel.rearrange("p (g e) -> p g e", e=GE)
            q = tmp.rearrange("p (n g) -> p n g", n=4)
            r = small.rearrange("p (n g) -> p n g", n=4)
            link(v.tensor_tensor(q[:, 0, :], s4[:, :, 0], s4[:, :, 1], ALU.max))
            link(v.tensor_tensor(q[:, 1, :], s4[:, :, 2], s4[:, :, 3], ALU.max))
            link(v.tensor_tensor(q[:, 2, :], s4[:, :, 0], s4[:, :, 1], ALU.min))
            link(v.tensor_tensor(q[:, 3, :], s4[:, :, 2], s4[:, :, 3], ALU.min))
            link(v.tensor_tensor(r[:, 0, :], q[:, 0, :], q[:, 1, :], ALU.max))
            link(v.tensor_tensor(r[:, 1, :], q[:, 0, :], q[:, 1, :], ALU.min))
            link(v.tensor_tensor(r[:, 2, :], q[:, 2, :], q[:, 3, :], ALU.max))
            link(v.tensor_tensor(r[:, 3, :], r[:, 1, :], r[:, 2, :], ALU.max))
            link(v.tensor_tensor(q[:, 0, :], r[:, 0, :], r[:, 3, :], ALU.add))

            best = rstd[:, :, 0]

            def first_largest(dst, scores, key, width, scratch):
                s3 = scores.rearrange("p (t e) -> p t e", t=TT)
                d3 = dst.rearrange("p (t e) -> p t e", t=TT)
                c3 = scratch.rearrange("p (t e) -> p t e", t=TT)
                wide = [P, TT, width]
                link(v.tensor_reduce(best, s3, AX_X, ALU.max))
                link(v.tensor_tensor(c3, s3, best.unsqueeze(2).to_broadcast(wide), ALU.is_equal))
                link(v.tensor_tensor(c3, c3, key, ALU.mult))
                link(v.tensor_reduce(best, c3, AX_X, ALU.max))
                link(v.tensor_tensor(d3, c3, best.unsqueeze(2).to_broadcast(wide), ALU.is_equal))

            first_largest(q[:, 1, :], q[:, 0, :], group_key[:], NG, q[:, 2, :])
            link(v.tensor_scalar(q[:, 3, :], q[:, 1, :], FAR, -FAR, ALU.mult, ALU.add))
            v4 = val.rearrange("p (g e) -> p g e", e=GE)
            wide = [P, TT * NG, GE]
            link(v.tensor_tensor(v4, s4, q[:, 1, :].unsqueeze(2).to_broadcast(wide), ALU.mult))
            link(v.tensor_tensor(v4, v4, q[:, 3, :].unsqueeze(2).to_broadcast(wide), ALU.add))
            first_largest(pick1, val, expert_key[:], E, tmp)
            link(v.scalar_tensor_tensor(out=val, in0=pick1, scalar=-2 * FAR, in1=val, op0=ALU.mult, op1=ALU.add))
            first_largest(pick2, val, expert_key[:], E, tmp)
            v.tensor_tensor(picks, pick1, pick2, ALU.add).then_inc(picks_ready, 1)
            dve.wait_ge(ranks_ready, 1)
            link(v.scalar_tensor_tensor(out=tmp, in0=psum[:, 1, 0:TT * E], scalar=1.0, in1=picks,
                                        op0=ALU.add, op1=ALU.mult))

            def block_ranks(b):
                link(v.tensor_scalar(rank[:, :, b * E:(b + 1) * E], t2(tmp), -1.0 - CAP * b, None, ALU.add))

            def place(it):
                now = rank[:, :, bass.ds(2 * it, 2)].unsqueeze(3).to_broadcast([P, TT, 2, CAP])
                v.tensor_tensor(one_hot[:], slot_no[:].rearrange("p (t i) s -> p t i s", t=TT), now,
                                ALU.is_equal).then_inc(onehot_ready, 1)

            link(v.tensor_reduce(best[:, 0:1], psum[:, 1, 2 * E:3 * E], AX_X, ALU.max))
            block_ranks(0)
            place(0)
            for b in range(1, BLOCKS + 1):
                block_ranks(b)
            v.tensor_scalar(overflow[:], best[:, 0:1], float(CAP), None, ALU.is_gt).then_inc(flag_ready, 1)
            sums = rstd
            for i, pick in enumerate((pick1, pick2)):
                link(v.tensor_tensor(tmp, pick, probs, ALU.mult))
                link(v.tensor_reduce(sums[:, :, 1 + i], t2(tmp), AX_X, ALU.add))
            link(v.tensor_tensor(best, sums[:, :, 1], sums[:, :, 2], ALU.add))
            link(v.reciprocal(best, best))
            for i, pick in enumerate((pick1, pick2)):
                link(v.tensor_tensor(sums[:, :, 1 + i], sums[:, :, 1 + i], best, ALU.mult))
                link(v.tensor_tensor(t2(pick), t2(pick), sums[:, :, 1 + i].unsqueeze(2).to_broadcast([P, TT, E]),
                                     ALU.mult))
            for b in range(BLOCKS + 1):
                link(v.tensor_tensor(gate[:, :, b * E:(b + 1) * E], t2(pick1), t2(pick2), ALU.add))
            def step(it):
                dve.wait_ge(onehot_ready, it + 1)
                now = gate[:, :, bass.ds(2 * it, 2)].unsqueeze(3).to_broadcast([P, TT, 2, CAP])
                v.tensor_tensor(one_hot_g[:], one_hot[:], now, ALU.mult).then_inc(gated_ready, 1)
                dve.wait_ge(gather_ready, 4 * it + 4)
                dve.wait_ge(gated_ready, it + 1)
                place(it + 1)
                dve.wait_ge(silu_ready, it + 1)
                dve.wait_ge(slots_free, STEP_CHUNKS * it + RING + 4)
                v.tensor_tensor(hidden, silu_h, psum[:, 1, :], ALU.mult).then_inc(hidden_ready, 1)
                for c in range(NC):
                    dve.wait_ge(comb_ready, 4 * it + c + 1)
                    cols = slice(c * CW, (c + 1) * CW)
                    v.tensor_tensor(area_a[:, 0, cols], area_a[:, 0, cols], psum[:, 6, :], ALU.add)
                    v.tensor_tensor(area_a[:, 1, cols], area_a[:, 1, cols], psum[:, 7, :],
                                    ALU.add).then_inc(comb_added, 1)
                    dve.wait_ge(comb_added, 4 * it + c + 1)
                    v.bn_stats(stats[:, 0, c, :], area_a[:, 0, cols])
                    v.bn_stats(stats[:, 1, c, :], area_a[:, 1, cols]).then_inc(stats_done, 1)

            dve.wait_ge(res_ready, TT)
            with dve.Fori(0, PAIRS) as it:
                step(it)
            dve.wait_ge(stats_done, NC * PAIRS)
            more = dve.value_load(overflow[0:1, 0:1], min_val=0, max_val=1)
            with dve.If(more > 0):
                with dve.Fori(PAIRS, BLOCKS * PAIRS) as it:
                    step(it)
                dve.wait_ge(stats_done, NC * PAIRS * BLOCKS)
            with dve.Else():
                dve.nop()

            for t in range(TT):
                link(v.bn_aggr(mv[:, t, :], stats[:, t]))
                variance(slice(t, t + 1))
            for t in range(TT):
                norm_scale(7 + t, t)
            scale_shift(2, y_out)


_INS = ["x", "ln_in_g", "ln_in_b", "w_in", "conv_a", "gate_ws", "gate_bs", "ln_v_g", "ln_v_b", "conv_c",
        "conv_c_b", "ln_c_g", "ln_c_b", "w_out", "ln1_g", "ln1_b", "w_router", "b_router", "w1", "w3", "w2",
        "ln2_g", "ln2_b"]


def kernel(**inputs):
    import numpy as _np
    import concourse.bacc as _bacc
    from concourse import mybir as _mybir
    from concourse.bass_utils import run_bass_kernel_spmd as _run

    nc = _bacc.Bacc("TRN2", target_bir_lowering=False, num_devices=1)
    arrays, args = {}, []
    for name in _INS:
        a = _np.ascontiguousarray(inputs[name])
        arrays[f"in_{name}_dram"] = a
        args.append(nc.dram_tensor(f"in_{name}_dram", a.shape, _mybir.dt.from_np(a.dtype), kind="ExternalInput").ap())
    shape = inputs["x"].shape
    args.append(nc.dram_tensor("out_0_dram", shape, _mybir.dt.float32, kind="ExternalOutput").ap())
    hybrid_layer(nc, *args)
    r = _run(nc, [arrays], core_ids=[0])
    return r.results[0]["out_0_dram"]
```

```python
from contextlib import ExitStack

import concourse.bass as bass
from concourse import mybir

P = 128
F32 = mybir.dt.float32
F32R = mybir.dt.float32r
I32 = mybir.dt.int32
ALU = mybir.AluOpType
ACT = mybir.ActivationFunctionType
AX_X = mybir.AxisListType.X
EPS = 1e-5
ALPHA = 2.0 ** 0.25
FAR = 1e30


def hybrid_layer(nc, x, ln_in_g, ln_in_b, w_in, conv_a, gate_ws, gate_bs, ln_v_g, ln_v_b,
                 conv_c, conv_c_b, ln_c_g, ln_c_b, w_out, ln1_g, ln1_b, w_router, b_router,
                 w1, w3, w2, ln2_g, ln2_b, out):
    _, SEQ, D = x.shape
    TT = SEQ // P
    KT = D // P
    TAPS_A, D_A = conv_a.shape[1:]
    TAPS_C, D_C = conv_c.shape[1:]
    HEADS = gate_ws.shape[1]
    BLK = gate_ws.shape[2]
    D_B = ln_v_g.shape[1]
    E = w_router.shape[1]
    FE = w1.shape[3]
    FT = FE // P
    CW = 512
    CT = CW // P
    NG, GE = 8, 4
    CAP = 64
    BLOCKS = SEQ // CAP
    PAIRS = E // 2
    NC = D // CW
    N_IN = w_in.shape[2] // CW
    N_OUT = NC
    N_MIX = N_IN + N_OUT
    STEP_UNITS = 12
    SLOTS = 8
    TWO = 2
    HALF = KT // 2
    ROW_A = TAPS_C + 3
    ROWS = ROW_A + 2 * TAPS_A
    PAD_A, PAD_C = TAPS_A - 1, TAPS_C - 1
    assert TT == 2 and BLK == P and D_A == 2 * CW and D_B == D_C == CW and HEADS == CT
    assert TWO * STEP_UNITS % SLOTS == 0 and PAIRS % TWO == 0
    UNIT = 4
    UNITS = KT // UNIT
    U_LEN = UNIT * CW
    UNIT_FLOATS = 2 * U_LEN
    assert UNIT_FLOATS == HALF * CW == TT * D
    N_UNITS = N_MIX * UNITS
    SPLITS = 3
    PRODUCTS = ((0, 0), (0, 1), (1, 0))

    GROUPS = KT // 4
    in_order = [t * GROUPS + q for q in range(GROUPS) for t in range(TT)]
    brought = {g: (e, n) for e, groups in enumerate(((0, 2, 3, 4, 6, 7), (1, 5))) for n, g in enumerate(groups)}

    def pool_lows(u):
        return u - u // UNITS

    B0, C0, XA0 = 0, D_A, 2 * D_A
    U0 = 3 * D_A
    V0, CA0, CG0 = U0 + D_B, U0 + 2 * D_B, U0 + 2 * D_B + D_C
    in_cols = [CA0, CG0, V0, U0] + [c + h * CW for h in range(2) for c in (C0, XA0, B0)]
    N_FIRST = 4
    assert len(in_cols) == N_IN

    with ExitStack() as ctx:
        def sb(name, shape, dt=F32):
            return ctx.enter_context(nc.sbuf_tensor(name, shape, dt))

        def sem(name):
            return ctx.enter_context(nc.semaphore(name))

        def aligned():
            return (nc.sbuf_base + 31) // 32 * 32

        ring_at = aligned()
        ring = sb("ring", [P, SLOTS - 2, UNIT_FLOATS])
        slot0 = sb("slot0", [P, UNIT_FLOATS])
        area_a = sb("area_a", [P, TT, D])
        area_b = sb("area_b", [P, TT, D])
        c_at = aligned()
        area_c = sb("area_c", [P, KT, SEQ])
        area_d = sb("area_d", [P, KT, SEQ])
        area_g = sb("area_g", [P, 2, D])
        psum = ctx.enter_context(nc.psum_tensor("psum", [P, 8, CW], F32))

        raw_bytes = 4 * 2 * UNIT_FLOATS
        w_part = [[nc.alloc_sbuf_tensor_at(f"w_{name}{b}", [P, UNIT, CW], F32R,
                                           offset=ring_at + raw_bytes + 4 * U_LEN * (2 * b + i))
                   for i, name in enumerate(("high", "low"))] for b in range(SPLITS)]
        in_part = [nc.alloc_sbuf_tensor_at("in_high", [P, KT, SEQ], F32R, offset=c_at),
                   nc.alloc_sbuf_tensor_at("in_low", [P, KT, SEQ], F32R,
                                           offset=ring_at + raw_bytes + 4 * U_LEN * 2 * SPLITS)]
        assert 4 * (U_LEN * 2 * SPLITS + KT * SEQ) <= 4 * 4 * UNIT_FLOATS

        def raw_unit(u):
            u = u % UNITS
            return ring[:, u // 2, (u % 2) * U_LEN:(u % 2 + 1) * U_LEN].rearrange("p (k c) -> p k c", k=UNIT)

        flat_a = area_a[:].rearrange("p t d -> p (t d)")
        flat_g = area_g[:].rearrange("p t d -> p (t d)")

        def quarter(flat, n):
            return flat[:, n * CT * SEQ:(n + 1) * CT * SEQ]

        plain = quarter(flat_a, 0).rearrange("p (c s) -> p c s", c=CT)
        sigm = quarter(flat_a, 1).rearrange("p (c s) -> p c s", c=CT)
        work = quarter(flat_a, 2).rearrange("p (c s) -> p c s", c=CT)
        v_rows = quarter(flat_a, 3).rearrange("p (k c) -> p k c", k=2)
        u_cm = quarter(flat_g, 0).rearrange("p (c s) -> p c s", c=CT)
        v_tm = quarter(flat_g, 1).rearrange("p (t c) -> p t c", t=TT)
        yc = quarter(flat_g, 2).rearrange("p (c s) -> p c s", c=CT)
        gate_shift = quarter(flat_g, 3)[:, 0:HEADS * BLK].rearrange("p (h i) -> p h i", h=HEADS)

        at = 0
        smalls = []
        for parts, width in ((CT, PAD_C + SEQ), (CT, PAD_A + SEQ), (1, CW), (CT, ROWS), (HEADS, BLK), (HEADS, BLK),
                             (1, P)):
            smalls.append(slot0[:, at:at + parts * width].rearrange("p (c s) -> p c s", c=parts))
            at += parts * width
        assert at <= UNIT_FLOATS
        glu, gated_x, rows_all, chan, ws_raw, ws_t, ln_all = smalls
        ln_rows = ln_all[0:2 * KT, 0, :]
        rows = rows_all[0:ROWS, 0, :]
        ln_chan = sb("ln_chan", [P, 4, KT])
        ident = sb("ident", [P, P])
        ones = sb("ones", [P, P])
        mean_w = sb("mean_w", [P, P])
        before = sb("before", [P, P])
        slot_no = sb("slot_no", [P, 2 * TT, CAP])
        group_key = sb("group_key", [P, TT, NG])
        expert_key = sb("expert_key", [P, TT, E])
        b_rt = sb("b_rt", [P, E])
        stats = sb("stats", [P, TT, NC, 6])
        mv = sb("mv", [P, TT, 2])
        rstd = sb("rstd", [P, TT, 4])
        v_stats = sb("v_stats", [P, TT, 6])
        c_rstd = sb("c_rstd", [P, 2, SEQ])
        rank = sb("rank", [P, TT, (BLOCKS + 1) * E])
        gate = sb("gate", [P, TT, (BLOCKS + 1) * E])
        one_hot = sb("one_hot", [P, TT, 2, CAP])
        one_hot_g = sb("one_hot_g", [P, TT, 2, CAP])
        one_hot_gt = sb("one_hot_gt", [P, TT, P])
        overflow = sb("overflow", [P, 1], I32)

        flat_d = area_d[:].rearrange("p k s -> p (k s)")
        y_sb = flat_d[:, 0:2 * CW].rearrange("p (b d) -> p b d", b=2)
        silu_h, hidden, hidden_2, rt_2 = (flat_d[:, n * CW:(n + 1) * CW] for n in (2, 3, 4, 7))
        hidden_t = hidden_2.rearrange("p (f s) -> p f s", f=FT)
        rt = rt_2.rearrange("p (n w) -> p n w", w=TT * E)
        ln2_scale = area_c[:].rearrange("p k s -> p (k s)")[:, D:2 * D]
        ln2_shift = [flat_d[:, 5 * CW:7 * CW], sb("ln2_shift1", [P, D // 2])[:]]
        w_rt, w_scaled = (ln2_shift[1][:, n * KT * E:(n + 1) * KT * E].rearrange("p (k e) -> p k e", k=KT)
                          for n in range(2))
        w_sums, logit_rows = (one_hot_g[:, t].rearrange("p r e -> p (r e)")[:, 0:2 * E].rearrange(
            "p (r e) -> p r e", r=2) for t in range(2))
        logit_bias = one_hot[:].rearrange("p t i s -> p (t i s)")[:, 0:TT * E]
        assert 2 * KT * E <= D // 2
        slots = [slot0[:]] + [ring[:, i, :] for i in range(SLOTS - 2)] + [flat_g]

        def slot(m):
            return slots[m % SLOTS].rearrange("p (i k f) -> p i k f", i=2, k=UNIT)

        gathered = area_c[:].rearrange("p k s -> p (k s)")[:, 0:KT * P].rearrange("p (k s) -> p k s", k=KT)

        s_rt, s_g2 = sem("router_weights_loaded"), sem("ln2_rows_loaded")
        s_x = [sem(f"x_loaded{t}") for t in range(TT)]
        s_small, s_ws, s_g, s_vrow, s_out = (
            sem(n) for n in ("rows_loaded", "ws_loaded", "ln_rows_loaded", "v_rows_loaded", "stored"))
        raw_loaded = [sem(f"raw_unit_loaded{i}") for i in range(UNITS)]
        s_ln, ln_turned, ln_chan_ready = sem("ln_rows_loaded_small"), sem("ln_rows_turned"), sem("ln_chan_ready")
        h_cm_ready = [sem(f"h_channel_major_ready{i}") for i in range(2)]
        first_low, in_low_pool = sem("first_low_half_ready"), sem("in_low_pool_ready")
        loaded = [sem(f"expert_unit_loaded{i}") for i in range(SLOTS)]
        high_ready, pool_low, dve_low = sem("high_ready"), sem("pool_low_ready"), sem("dve_low_ready")
        in_high, in_low = sem("in_high_ready"), sem("in_low_ready")
        consts = sem("consts_ready")
        units_done = sem("units_done")
        experts_done = sem("expert_units_done")
        drained = [sem(f"psum_drained{i}") for i in range(3)]
        extra_ready, extra_drained = sem("extra_ready"), sem("extra_drained")
        dve_step = sem("dve_step")
        var_ready, root_ready = sem("var_ready"), sem("root_ready")
        scale_ready, normed, stats_done = sem("norm_scale_ready"), sem("normed"), sem("stats_done")
        h0_ready, vn_ready, conv_c_step = sem("h0_ready"), sem("vn_ready"), sem("conv_c_step")
        z_ready, z_used, y_b_done = sem("z_ready"), sem("z_used"), sem("y_b_done")
        c_mean, c_sq, c_var, c_varused, c_norm, yc_done = (
            sem(n) for n in ("c_mean_ready", "c_squares_ready", "c_var_ready", "c_var_used", "c_normed", "y_c_done"))
        conv_step = sem("conv_a_step")
        x1_ready = sem("scaled_x1_ready")
        w_sums_ready, rows_summed, rows_kept = sem("w_sums_ready"), sem("rows_summed"), sem("rows_kept")
        r_turned, r_kept, logits_fixed = sem("sums_turned"), sem("sums_kept"), sem("logits_fixed")
        logits_ready, probs_ready, picks_ready, ranks_ready = (
            sem(n) for n in ("logits_ready", "probs_ready", "picks_ready", "ranks_ready"))
        flag_ready = sem("flag_ready")
        onehot_ready, gated_ready = sem("onehot_ready"), sem("gated_onehot_ready")
        gather_ready, gather_drained = sem("gather_ready"), sem("gather_drained")
        silu_ready, hidden_ready = sem("silu_ready"), sem("hidden_ready")
        ht_ready, ht_drained = sem("hidden_t_ready"), sem("hidden_t_drained")
        gt_ready, gt_drained = sem("onehot_t_ready"), sem("onehot_t_drained")
        y_ready, y_drained = sem("y_ready"), sem("y_drained")
        comb_ready, comb_added = sem("combined_ready"), sem("combined_added")
        y_out, y_out_scaled, y_out_pool = sem("y_out"), sem("y_out_scaled"), sem("y_out_pool")

        def chunk_psum(n):
            b = 2 * (n % 3)
            return psum[:, b:b + 2, :]

        def channel_psum(n):
            return chunk_psum(n).rearrange("p b (c s) -> p (b c) s", s=SEQ)

        def spread(row):
            return row.partition_broadcast(P)

        block = ctx.enter_context(nc.Block())

        @block.sync
        def _(sp):
            for t in range(TT):
                sp.dma_start(area_a[:, t, :], x[0, t * P:(t + 1) * P, :]).then_inc(s_x[t], 16)
                if t == 0:
                    for r, src in enumerate((ln_in_g, ln_in_b)):
                        sp.dma_start(ln_rows[r * KT:(r + 1) * KT, :],
                                     src.rearrange("(k p) -> k p", p=P)).then_inc(s_ln, 16)

            for u in range(N_UNITS):
                n, q = divmod(u, UNITS)
                if n < N_IN:
                    src = w_in[0][:, in_cols[n]:in_cols[n] + CW]
                else:
                    src = w_out[0][:, (n - N_IN) * CW:(n - N_IN + 1) * CW]
                if u >= UNITS:
                    if u == UNITS:
                        sp.wait_ge(first_low, 1)
                    if q < UNITS - 1:
                        sp.wait_ge(pool_low, pool_lows(u - UNITS + 1))
                    else:
                        sp.wait_ge(dve_low, n)
                sp.dma_start(raw_unit(u), src.rearrange("(q k p) c -> q p k c", q=UNITS, p=P)[q]).then_inc(
                    raw_loaded[q], 16)
                if u == UNITS - 1:
                    sp.dma_start(area_g[:, 0, :], spread(ln_in_g)).then_inc(s_g, 16)
                    sp.dma_start(area_g[:, 1, :], spread(ln_in_b)).then_inc(s_g, 16)
            sp.wait_ge(units_done, UNITS * (N_IN + 1))
            sp.dma_start(area_g[:, 0, :], spread(ln1_g[0])).then_inc(s_g, 16)
            sp.dma_start(area_g[:, 1, :], spread(ln1_b[0])).then_inc(s_g, 16)

            def load_expert_unit(m, j, pair):
                for i in range(2):
                    e = 2 * pair + i
                    if j < 8:
                        src = (w1, w3)[j // 4][0, e].rearrange("(q k p) f -> q p k f", q=4, p=P)[j % 4]
                    else:
                        src = w2[0, e].rearrange("(f p) (c d) -> c p f d", p=P, c=NC)[j - 8]
                    sp.dma_start(slot(m)[:, i], src).then_inc(loaded[m % SLOTS], 16)

            load_expert_unit(0, 0, 0)
            sp.wait_ge(pool_low, pool_lows(N_UNITS - 2))
            load_expert_unit(1, 1, 0)
            sp.wait_ge(pool_low, pool_lows(N_UNITS))
            sp.wait_ge(dve_low, N_MIX)
            load_expert_unit(2, 2, 0)
            sp.wait_ge(units_done, N_UNITS)
            for m in range(3, SLOTS - 1):
                load_expert_unit(m, m, 0)
            sp.wait_ge(logits_ready, 1)
            sp.dma_start(ln2_scale, spread(ln2_g[0])).then_inc(s_g2, 16)
            for h in range(2):
                sp.dma_start(ln2_shift[h], spread(ln2_b[0][h * D // 2:(h + 1) * D // 2])).then_inc(s_g2, 16)
            sp.wait_ge(x1_ready, 2 * TT)
            load_expert_unit(SLOTS - 1, SLOTS - 1, 0)
            with sp.Fori(0, PAIRS // TWO - 1) as i2:
                for n in range(SLOTS, SLOTS + TWO * STEP_UNITS):
                    sp.wait_ge(experts_done, TWO * STEP_UNITS * i2 + n - SLOTS + 1)
                    load_expert_unit(n, n % STEP_UNITS, TWO * i2 + n // STEP_UNITS)
            for m in range((PAIRS - TWO) * STEP_UNITS + SLOTS, PAIRS * STEP_UNITS):
                sp.wait_ge(experts_done, m - SLOTS + 1)
                load_expert_unit(m, m % STEP_UNITS, m // STEP_UNITS)
            sp.wait_ge(flag_ready, 1)
            more = sp.value_load(overflow[0:1, 0:1], min_val=0, max_val=1)
            with sp.If(more > 0):
                with sp.Fori(1, BLOCKS) as b:
                    with sp.Fori(0, PAIRS // TWO) as i2:
                        for n in range(TWO * STEP_UNITS):
                            sp.wait_ge(experts_done, PAIRS * STEP_UNITS * b + TWO * STEP_UNITS * i2 + (n - SLOTS + 1))
                            load_expert_unit(n, n % STEP_UNITS, TWO * i2 + n // STEP_UNITS)
                sp.nop()
            with sp.Else():
                sp.nop()
            for t in range(TT):
                for h in range(2):
                    if 2 * t + h < 2 * TT - 1:
                        sp.wait_ge(y_out, 2 * t + h + 1)
                    else:
                        sp.wait_ge(y_out_pool, 1)
                    cols = slice(h * D // 2, (h + 1) * D // 2)
                    sp.dma_start(out[0, t * P:(t + 1) * P, cols], area_b[:, t, cols]).then_inc(s_out, 16)
            sp.wait_ge(s_out, 16 * 2 * TT)

        @block.gpsimd
        def _(pool):
            nc.gpsimd.memset(ones[:], 1.0).then_inc(consts, 1)
            nc.gpsimd.memset(mean_w[:], 1.0 / D_C).then_inc(consts, 1)
            pool.wait_ge(consts, 1)
            nc.gpsimd.affine_select(out=ident[:], in_=ones[:], compare_op=ALU.is_equal, fill=0.0, base=0,
                                    pattern=[[-1, P]], channel_multiplier=1).then_inc(consts, 1)
            nc.gpsimd.affine_select(out=before[:], in_=ones[:], compare_op=ALU.is_gt, fill=0.0, base=0,
                                    pattern=[[1, P]], channel_multiplier=-1).then_inc(consts, 1)
            nc.gpsimd.iota(slot_no[:], pattern=[[0, 2 * TT], [1, CAP]], base=0, channel_multiplier=0,
                           allow_small_or_imprecise_dtypes=True).then_inc(consts, 1)
            nc.gpsimd.iota(group_key[:], pattern=[[0, TT], [-1, NG]], base=NG, channel_multiplier=0,
                           allow_small_or_imprecise_dtypes=True).then_inc(consts, 1)
            nc.gpsimd.iota(expert_key[:], pattern=[[0, TT], [-1, E]], base=E, channel_multiplier=0,
                           allow_small_or_imprecise_dtypes=True).then_inc(consts, 1)
            nc.gpsimd.memset(glu[:, :, 0:PAD_C], 0.0).then_inc(consts, 1)
            nc.gpsimd.memset(gated_x[:, :, 0:PAD_A], 0.0).then_inc(consts, 1)
            pool.wait_ge(consts, 9)
            nc.gpsimd.memset(ws_t[P // 2:P, :, 0:BLK // 2], 0.0).then_inc(consts, 1)

            def input_low(k):
                pool.wait_ge(in_high, TT * k + 1)
                tiles = slice(4 * k, 4 * k + 4)
                nc.gpsimd.tensor_tensor(in_part[1][:, tiles, 0:P], area_d[:, tiles, 0:P],
                                        in_part[0][:, tiles, 0:P].bitcast(F32), ALU.subtract).then_inc(in_low_pool, 1)

            input_low(0)
            for u in range(N_UNITS):
                if u == 1:
                    for k in range(1, GROUPS):
                        input_low(k)
                if u % UNITS < UNITS - 1:
                    pool.wait_ge(high_ready, u + 1)
                    high, low = w_part[u % SPLITS]
                    tiles = slice(0, UNIT // 2 if u == 0 else UNIT)
                    nc.gpsimd.tensor_tensor(low[:, tiles], raw_unit(u)[:, tiles], high[:, tiles].bitcast(F32),
                                            ALU.subtract).then_inc(pool_low, 1)
            pool.wait_ge(normed, 2 * TT * 2 + 1)
            pool.wait_ge(s_g2, 16 * 3)
            last = area_b[:, TT - 1, D // 2:]
            nc.gpsimd.tensor_tensor(last, last, ln2_scale[:, D // 2:], ALU.mult).then_inc(y_out_scaled, 1)
            pool.wait_ge(y_out_scaled, 1)
            nc.gpsimd.tensor_tensor(last, last, ln2_shift[1], ALU.add).then_inc(y_out_pool, 1)
        CONSTS = 10

        @block.tensor
        def _(pe):
            pe.wait_ge(consts, CONSTS)
            def turn_rows(ready, t):
                for g in range(KT // 4):
                    if g % 2 == 0:
                        pe.wait_ge(ready, 2 * t + g // 2 + 1)
                    for j in range(4):
                        k = 4 * g + j
                        mm = pe.transpose(psum[:, 4 * t + g, j * P:(j + 1) * P],
                                          area_b[:, t, k * P:(k + 1) * P], ident[:])
                    mm.then_inc(extra_ready, 1)

            pe.wait_ge(s_ln, 16 * 2)
            pe.transpose(psum[:, 7, 0:2 * KT], ln_rows, ident[0:2 * KT, 0:2 * KT]).then_inc(ln_turned, 1)
            turn_rows(normed, 0)
            pe.wait_ge(ln_chan_ready, 1)
            turn_rows(normed, 1)

            def unit(u):
                pe.wait_ge(high_ready, u + 1)
                if u == 0:
                    pe.wait_ge(first_low, 1)
                if u % UNITS < UNITS - 1:
                    pe.wait_ge(pool_low, pool_lows(u + 1))
                else:
                    pe.wait_ge(dve_low, u // UNITS + 1)
                return w_part[u % SPLITS]

            def channels(n):
                if n >= 3:
                    pe.wait_ge(drained[n % 3], n // 3)
                o = channel_psum(n)
                for q in range(UNITS):
                    w = unit(UNITS * n + q)
                    if n == 0:
                        pe.wait_ge(in_high, TT * (q + 1))
                        pe.wait_ge(in_low_pool, q + 1)
                        pe.wait_ge(in_low, q + 1)
                    for k in range(UNIT):
                        kk = UNIT * q + k
                        for c in range(CT):
                            for a, b in PRODUCTS:
                                mm = pe.matmul(o[:, c, :], w[a][:, k, c * P:(c + 1) * P], in_part[b][:, kk, :],
                                               start=kk == 0 and a + b == 0 and c % 2 == 0,
                                               stop=kk == KT - 1 and a == 1, skip_group_check=True)
                    mm.then_inc(units_done, 1)

            def tokens(n):
                if n >= 3:
                    pe.wait_ge(drained[n % 3], n // 3)
                o = chunk_psum(n)
                for q in range(UNITS):
                    w = unit(UNITS * n + q)
                    if n == N_IN:
                        pe.wait_ge(in_high, TT * KT // 4 + q + 1)
                        pe.wait_ge(in_low, GROUPS + q + 1)
                    for k in range(UNIT):
                        kk = UNIT * q + k
                        for t in range(TT):
                            for a, b in PRODUCTS:
                                mm = pe.matmul(o[:, t, :], in_part[a][:, kk, t * P:(t + 1) * P], w[b][:, k, :],
                                               start=kk == 0 and a + b == 0, stop=kk == KT - 1 and a == 1)
                    mm.then_inc(units_done, 1)

            channels(0)
            pe.wait_ge(s_small, 16 * 6)
            for c in range(CT):
                mm = pe.transpose(psum[:, 6, c * ROWS:(c + 1) * ROWS], rows[:, c * P:(c + 1) * P],
                                  ident[0:ROWS, 0:ROWS])
            pe.wait_ge(s_ln, 16 * 4)
            pe.transpose(psum[:, 6, CT * ROWS:CT * ROWS + 2 * KT], ln_rows,
                         ident[0:2 * KT, 0:2 * KT]).then_inc(extra_ready, 1)
            pe.wait_ge(s_ws, 16)
            for h in range(HEADS):
                mm = pe.transpose(psum[:, 7, h * P:(h + 1) * P], ws_raw[:, h, :], ident[:])
            mm.then_inc(extra_ready, 1)
            channels(1)
            tokens(2)
            channels(3)
            channels(4)
            pe.wait_ge(vn_ready, 1)
            z = psum[:, 6:8, :].rearrange("p b (h s) -> p (b h) s", s=SEQ)
            for h in range(HEADS):
                for t in range(TT):
                    mm = pe.matmul(z[:, h, t * P:(t + 1) * P], v_tm[:, t, h * P:(h + 1) * P], ws_t[:, h, :],
                                   start=True, stop=True)
            mm.then_inc(z_ready, 1)
            channels(5)
            channels(6)
            pe.wait_ge(z_used, 1)
            pe.wait_ge(conv_c_step, TAPS_C * CT)
            for c in range(CT):
                mm = pe.matmul(psum[:, 6, 0:SEQ], mean_w[:], yc[:, c, :], start=c == 0, stop=c == CT - 1)
            mm.then_inc(c_mean, 1)
            channels(7)
            pe.wait_ge(c_sq, 1)
            for c in range(CT):
                mm = pe.matmul(psum[:, 7, 0:SEQ], mean_w[:], sigm[:, c, :], start=c == 0, stop=c == CT - 1)
            mm.then_inc(c_var, 1)
            channels(8)
            channels(9)
            pe.wait_ge(w_sums_ready, 1)
            pe.matmul(psum[:, 6, 0:2 * E], ones[:], w_sums.rearrange("p r e -> p (r e)"),
                      start=True, stop=True).then_inc(rows_summed, 1)

            def turn_sums(c):
                n = N_IN + c
                pe.wait_ge(drained[n % 3], n // 3 + 1)
                if c == 0:
                    pe.wait_ge(rows_kept, 1)
                    pe.wait_ge(c_varused, 1)
                else:
                    pe.wait_ge(r_kept, TT * c)
                for t in range(TT):
                    for j in range(CT):
                        at = c * CW + j * P
                        mm = pe.transpose(psum[:, 6 + t, j * P:(j + 1) * P], area_a[:, t, at:at + P], ident[:])
                    mm.then_inc(r_turned, 1)

            def logits(c):
                if c == 0:
                    pe.wait_ge(drained[2], 4)
                pe.wait_ge(r_kept, TT * (c + 1))
                for j in range(CT):
                    k = CT * c + j
                    for t in range(TT):
                        mm = pe.matmul(psum[:, 4, t * E:(t + 1) * E], area_d[:, k, t * P:(t + 1) * P],
                                       w_scaled[:, k, :], start=k == 0 and t == 0, stop=k == KT - 1,
                                       skip_group_check=True)
                return mm

            tokens(N_IN)
            tokens(N_IN + 1)
            turn_sums(0)
            tokens(N_IN + 2)
            turn_sums(1)
            logits(0)
            tokens(N_IN + 3)
            turn_sums(2)
            logits(1)
            logits(2)
            turn_sums(3)
            logits(3).then_inc(logits_ready, 1)
            pe.wait_ge(picks_ready, 1)
            picks = rt[:, 5, :].rearrange("p (t e) -> p t e", t=TT)
            pe.matmul(psum[:, 1, 0:E], before[:], picks[:, 0, :], start=True, stop=True)
            pe.matmul(psum[:, 1, E:2 * E], ones[:], picks[:, 0, :], start=True, stop=False)
            pe.matmul(psum[:, 1, E:2 * E], before[:], picks[:, 1, :], start=False, stop=True)
            pe.matmul(psum[:, 1, 2 * E:3 * E], ones[:], picks[:, 0, :], start=True, stop=False)
            pe.matmul(psum[:, 1, 2 * E:3 * E], ones[:], picks[:, 1, :], start=False, stop=True).then_inc(ranks_ready, 1)

            def gather(it, g):
                for j in range(4):
                    k = 4 * g + j
                    for t in range(TT):
                        mm = pe.matmul(psum[:, 2 + g % 2, j * P:(j + 1) * P],
                                       area_b[:, t, k * P:(k + 1) * P],
                                       one_hot[:, t].rearrange("p i s -> p (i s)"),
                                       start=t == 0, stop=t == TT - 1)
                mm.then_inc(gather_ready, 1)

            def step(i2, s):
                it = TWO * i2 + s

                def arrived(j):
                    n = STEP_UNITS * s + j
                    fills = TWO * STEP_UNITS // SLOTS
                    pe.wait_ge(loaded[n % SLOTS], 32 * fills * i2 + 32 * (n // SLOTS + 1))
                    return slot(n)

                for j in range(2 * UNITS):
                    if j < 2:
                        pe.wait_ge(gather_drained, 4 * it + j + 1)
                        gather(it, 2 + j)
                    elif j < UNITS:
                        pe.wait_ge(gather_drained, 4 * it + j + 1)
                    w = arrived(j)
                    for k in range(UNIT):
                        kk = UNIT * (j % UNITS) + k
                        for i in range(2):
                            mm = pe.matmul(psum[i * CAP:(i + 1) * CAP, j // UNITS, :],
                                           gathered[:, kk, i * CAP:(i + 1) * CAP], w[:, i, k, :],
                                           start=kk == 0, stop=kk == KT - 1)
                    mm.then_inc(experts_done, 1)
                pe.wait_ge(onehot_ready, it + 2)
                gather(it + 1, 0)
                gather(it + 1, 1)
                pe.wait_ge(hidden_ready, it + 1)
                pe.wait_ge(gather_drained, 4 * it + 5)
                for f in range(FT):
                    mm = pe.transpose(psum[:, 2, f * P:(f + 1) * P], hidden[:, f * P:(f + 1) * P], ident[:])
                mm.then_inc(ht_ready, 1)
                pe.wait_ge(gated_ready, it + 1)
                pe.wait_ge(gather_drained, 4 * it + 6)
                for t in range(TT):
                    mm = pe.transpose(psum[:, 3, t * P:(t + 1) * P],
                                      one_hot_g[:, t].rearrange("p i s -> p (i s)"), ident[:])
                mm.then_inc(gt_ready, 1)
                pe.wait_ge(ht_drained, it + 1)

                def project(c):
                    w = arrived(2 * UNITS + c)
                    if c >= 2:
                        pe.wait_ge(y_drained, 4 * it + c - 1)
                    for f in range(FT):
                        for i in range(2):
                            mm = pe.matmul(psum[i * CAP:(i + 1) * CAP, 4 + c % 2, :],
                                           hidden_t[:, f, i * CAP:(i + 1) * CAP], w[:, i, f, :],
                                           start=f == 0, stop=f == FT - 1)
                            if c == 1 and f == 0 and i == 0:
                                mm.then_inc(experts_done, 1)
                    mm.then_inc(y_ready, 1)

                def combine(c):
                    pe.wait_ge(y_drained, 4 * it + c + 1)
                    if c == 0:
                        pe.wait_ge(gt_drained, it + 1)
                    else:
                        pe.wait_ge(comb_added, 4 * it + c)
                    for t in range(TT):
                        mm = pe.matmul(psum[:, 6 + t, :], one_hot_gt[:, t, :], y_sb[:, c % 2, :],
                                       start=True, stop=True)
                        if t == 0 and c != NC - 2:
                            mm.then_inc(experts_done, 1)
                    mm.then_inc(comb_ready, 1)

                project(0)
                project(1)
                combine(0)
                project(2)
                combine(1)
                combine(2)
                project(3)
                combine(3)

            pe.wait_ge(normed, 2 * TT * 2)
            pe.wait_ge(onehot_ready, 1)
            gather(0, 0)
            gather(0, 1)
            with pe.Fori(0, PAIRS // TWO) as i2:
                for s in range(TWO):
                    step(i2, s)
            pe.wait_ge(flag_ready, 1)
            more = pe.value_load(overflow[0:1, 0:1], min_val=0, max_val=1)
            with pe.If(more > 0):
                with pe.Fori(PAIRS // TWO, BLOCKS * PAIRS // TWO) as i2:
                    for s in range(TWO):
                        step(i2, s)
                pe.nop()
            with pe.Else():
                pe.nop()

        @block.scalar
        def _(act):
            act.dma_start(rows[0:TAPS_C, :], conv_c[0]).then_inc(s_small, 16)
            for r, src in enumerate((conv_c_b, ln_c_g, ln_c_b)):
                act.dma_start(rows[TAPS_C + r:TAPS_C + r + 1, :], src).then_inc(s_small, 16)
            for h in range(2):
                act.dma_start(rows[ROW_A + h * TAPS_A:ROW_A + (h + 1) * TAPS_A, :],
                              conv_a[0][:, h * CW:(h + 1) * CW]).then_inc(s_small, 16)
            act.dma_start(ws_raw[:], gate_ws[0].rearrange("h i j -> i h j")).then_inc(s_ws, 16)
            act.dma_start(b_rt[:], spread(b_router)).then_inc(s_vrow, 16)
            act.dma_start(w_rt, w_router.rearrange("(k p) e -> p k e", p=P)).then_inc(s_rt, 16)

            def root(n, t):
                act.wait_ge(var_ready, n)
                act.activation(rstd[:, t, 1], rstd[:, t, 0], ACT.Sqrt).then_inc(root_ready, 1)

            def normalise_tile(n, t):
                act.wait_ge(scale_ready, TT * n + t + 1)
                for h in range(2):
                    cols = slice(h * D // 2, (h + 1) * D // 2)
                    act.activation(area_b[:, t, cols], area_a[:, t, cols], ACT.Identity,
                                   scale=rstd[:, t, 2:3], bias=rstd[:, t, 3:4]).then_inc(normed, 1)

            def high(u):
                act.wait_ge(raw_loaded[u % UNITS], 16 * (u // UNITS + 1))
                if u >= SPLITS:
                    act.wait_ge(units_done, u - SPLITS + 1)
                act.activation(w_part[u % SPLITS][0][:], raw_unit(u), ACT.Copy).then_inc(high_ready, 1)

            def input_plain(g):
                t, k = divmod(4 * g, KT)
                act.wait_ge(extra_ready, g + 1)
                for j in range(4):
                    ins = act.activation(area_d[:, k + j, t * P:(t + 1) * P], psum[:, g, j * P:(j + 1) * P],
                                         ACT.Identity, scale=ln_chan[:, 0, k + j:k + j + 1],
                                         bias=ln_chan[:, 1, k + j:k + j + 1])
                ins.then_inc(h_cm_ready[1], 1)

            def input_high(g):
                t, k = divmod(4 * g, KT)
                e, n = brought[g]
                act.wait_ge(h_cm_ready[e], n + 1)
                at = slice(k, k + 4), slice(t * P, (t + 1) * P)
                act.activation(in_part[0][:, at[0], at[1]], area_d[:, at[0], at[1]], ACT.Copy).then_inc(in_high, 1)

            root(1, slice(0, 1))
            normalise_tile(0, 0)
            act.wait_ge(ln_turned, 1)
            act.activation(ln_chan[:, 0:2], psum[:, 7, 0:2 * KT].rearrange("p (r k) -> p r k", r=2),
                           ACT.Copy).then_inc(ln_chan_ready, 1)
            for r, src in enumerate((ln1_g[0], ln1_b[0])):
                act.dma_start(ln_rows[r * KT:(r + 1) * KT, :],
                              src.rearrange("(k p) -> k p", p=P)).then_inc(s_ln, 16)
            act.wait_ge(ln_chan_ready, 1)
            input_plain(1)
            root(2, slice(1, 2))
            normalise_tile(0, 1)
            for g in in_order:
                if g == 5:
                    input_plain(5)
                input_high(g)
                if g == 0:
                    high(0)

            def load_rows():
                act.wait_ge(h0_ready, 2 * TT)
                act.dma_start(v_rows[:, 0, :], spread(ln_v_g[0])).then_inc(s_vrow, 16)
                act.dma_start(v_rows[:, 1, :], spread(ln_v_b[0])).then_inc(s_vrow, 16)
                act.dma_start(gate_shift, spread(gate_bs[0])).then_inc(s_vrow, 16)

            def keep_small():
                act.wait_ge(extra_ready, TT * KT // 4 + 1)
                act.activation(chan[:], psum[:, 6, 0:CT * ROWS].rearrange("p (c r) -> p c r", c=CT),
                               ACT.Copy).then_inc(extra_drained, 1)
                act.activation(ln_chan[:, 2:4], psum[:, 6, CT * ROWS:CT * ROWS + 2 * KT].rearrange(
                    "p (r k) -> p r k", r=2), ACT.Copy).then_inc(extra_drained, 1)
                act.wait_ge(extra_ready, TT * KT // 4 + 2)
                wsp = psum[:, 7, :].rearrange("p (h i) -> p h i", h=HEADS)
                act.activation(ws_t[0:P // 2], wsp[0:P // 2], ACT.Copy)
                act.activation(ws_t[P // 2:P, :, BLK // 2:], wsp[P // 2:P, :, BLK // 2:],
                               ACT.Copy).then_inc(extra_drained, 1)

            def after_chunk(n):
                act.wait_ge(units_done, UNITS * (n + 1))
                if n == 0:
                    act.activation(plain, channel_psum(n), ACT.Copy).then_inc(drained[0], 1)
                elif n == 1:
                    act.activation(sigm, channel_psum(n), ACT.Sigmoid).then_inc(drained[1], 1)
                elif n == 3:
                    act.activation(u_cm, channel_psum(n), ACT.Copy).then_inc(drained[0], 1)
                elif n == 4 or n == 7:
                    if n == 4:
                        act.wait_ge(conv_c_step, CT)
                    else:
                        act.wait_ge(drained[2], 2)
                    act.activation(plain, channel_psum(n), ACT.Copy).then_inc(drained[1], 1)
                elif n == 8:
                    act.wait_ge(c_norm, 1)
                    for c in range(CT):
                        act.activation(area_d[:, 12 + c, :], yc[:, c, :], ACT.Silu,
                                       scale=chan[:, c, TAPS_C + 1:TAPS_C + 2],
                                       bias=chan[:, c, TAPS_C + 2:TAPS_C + 3]).then_inc(yc_done, 1)
                elif n == N_IN - 1:
                    for q in range(UNITS):
                        if q == 1:
                            act.wait_ge(drained[0], 4)
                        elif q == 2:
                            act.wait_ge(y_b_done, 1)
                        rows_q = slice(4 * q, 4 * q + 4)
                        act.activation(in_part[0][:, rows_q, :], area_d[:, rows_q, :],
                                       ACT.Copy).then_inc(in_high, 1)

            def keep_sums(c):
                for t in range(TT):
                    act.wait_ge(r_turned, TT * c + t + 1)
                    act.activation(area_d[:, CT * c:CT * (c + 1), t * P:(t + 1) * P],
                                   psum[:, 6 + t, :].rearrange("p (j s) -> p j s", j=CT),
                                   ACT.Copy).then_inc(r_kept, 1)

            for u in range(1, N_UNITS):
                high(u)
                if u == UNITS - 1:
                    load_rows()
                if u == UNITS + 2:
                    keep_small()
                if u == 4 * UNITS - 1:
                    root(3, slice(0, TT))
                if u == 9 * UNITS - 1:
                    act.wait_ge(c_varused, 1)
                    act.activation(c_rstd[:, 1, :], c_rstd[:, 0, :], ACT.Sqrt).then_inc(root_ready, 1)
                if u == UNITS * N_IN + 2:
                    act.wait_ge(rows_summed, 1)
                    act.activation(logit_rows, psum[:, 6, 0:2 * E].rearrange("p (r e) -> p r e", r=2),
                                   ACT.Copy).then_inc(rows_kept, 1)
                for c in range(2):
                    if u == UNITS * (N_IN + 2 + c) + 2:
                        keep_sums(c)
                n, q = divmod(u - 1, UNITS)
                if q == 0 and 1 <= n <= N_IN:
                    after_chunk(n - 1)

            keep_sums(2)
            root(4, slice(0, TT))
            keep_sums(3)
            normalise_tile(1, 0)
            act.wait_ge(logits_fixed, 1)
            act.activation(rt[:, 0, :], rt[:, 7, :], ACT.Sigmoid).then_inc(probs_ready, 1)
            normalise_tile(1, 1)

            def keep_gathered(it, groups):
                for g in groups:
                    act.wait_ge(gather_ready, 4 * it + g + 1)
                    for k in range(4 * g, 4 * g + 4):
                        ins = act.activation(gathered[:, k, :], psum[:, 2 + g % 2, k % 4 * P:(k % 4 + 1) * P],
                                             ACT.Identity, scale=ln_chan[:, 2, k:k + 1], bias=ln_chan[:, 3, k:k + 1])
                    ins.then_inc(gather_drained, 1)

            def step(it):
                keep_gathered(it, (2, 3))
                act.wait_ge(experts_done, STEP_UNITS * it + UNITS)
                act.activation(silu_h, psum[:, 0, :], ACT.Silu).then_inc(silu_ready, 1)
                keep_gathered(it + 1, (0, 1))
                act.wait_ge(ht_ready, it + 1)
                act.activation(hidden_t, psum[:, 2, :].rearrange("p (f s) -> p f s", f=FT),
                               ACT.Copy).then_inc(ht_drained, 1)
                act.wait_ge(gt_ready, it + 1)
                act.activation(one_hot_gt[:], psum[:, 3, 0:TT * P].rearrange("p (t s) -> p t s", t=TT),
                               ACT.Copy).then_inc(gt_drained, 1)
                for c in range(NC):
                    act.wait_ge(y_ready, 4 * it + c + 1)
                    if c >= 2:
                        act.wait_ge(comb_ready, 4 * it + c - 1)
                    act.activation(y_sb[:, c % 2, :], psum[:, 4 + c % 2, :],
                                   ACT.Copy).then_inc(y_drained, 1)

            keep_gathered(0, (0, 1))
            with act.Fori(0, PAIRS) as it:
                step(it)
            act.wait_ge(flag_ready, 1)
            more = act.value_load(overflow[0:1, 0:1], min_val=0, max_val=1)
            with act.If(more > 0):
                with act.Fori(PAIRS, BLOCKS * PAIRS) as it:
                    step(it)
                act.nop()
            with act.Else():
                act.nop()
            root(5, slice(0, TT))
            act.wait_ge(scale_ready, TT * 3)
            act.activation(area_b[:, TT - 1, D // 2:], area_a[:, TT - 1, D // 2:], ACT.Identity,
                           scale=rstd[:, TT - 1, 2:3], bias=rstd[:, TT - 1, 3:4]).then_inc(normed, 1)

        @block.vector
        def _(dve):
            v = nc.vector
            steps = [0]

            def link(ins):
                steps[0] += 1
                ins.then_inc(dve_step, 1)
                dve.wait_ge(dve_step, steps[0])

            def variance(t):
                v.tensor_scalar(rstd[:, t, 0], mv[:, t, 1], EPS, None, ALU.add).then_inc(var_ready, 1)

            def inverse_root(n, t):
                dve.wait_ge(root_ready, n)
                link(v.reciprocal(rstd[:, t, 2], rstd[:, t, 1]))

            def norm_scale(n, one):
                inverse_root(n, one)
                v.scalar_tensor_tensor(out=rstd[:, one, 3], in0=mv[:, one, 0], scalar=-1.0, in1=rstd[:, one, 2],
                                       op0=ALU.mult, op1=ALU.mult).then_inc(scale_ready, one.stop - one.start)

            def scale_shift(ready):
                dve.wait_ge(s_g, 32)
                for t in range(TT):
                    for h in range(2):
                        cols = slice(h * D // 2, (h + 1) * D // 2)
                        dst = area_b[:, t, cols]
                        dve.wait_ge(normed, 2 * t + h + 1)
                        link(v.tensor_tensor(dst, dst, area_g[:, 0, cols], ALU.mult))
                        v.tensor_tensor(dst, dst, area_g[:, 1, cols], ALU.add).then_inc(ready, 1)

            for t in range(TT):
                dve.wait_ge(s_x[t], 16)
                for c in range(NC):
                    link(v.bn_stats(stats[:, t, c, :], area_a[:, t, c * CW:(c + 1) * CW]))
                    if t == 1 and c == 0:
                        norm_scale(1, slice(0, 1))
                link(v.bn_aggr(mv[:, t, :], stats[:, t]))
                variance(slice(t, t + 1))
            norm_scale(2, slice(1, 2))
            dve.wait_ge(ln_chan_ready, 1)

            def input_low(q):
                tiles = slice(4 * q, 4 * q + 4)
                dve.wait_ge(in_high, TT * (q + 1))
                v.tensor_tensor(in_part[1][:, tiles, P:SEQ], area_d[:, tiles, P:SEQ],
                                in_part[0][:, tiles, P:SEQ].bitcast(F32), ALU.subtract).then_inc(in_low, 1)

            def input_plain(g):
                t, k = divmod(4 * g, KT)
                dve.wait_ge(extra_ready, g + 1)
                for j in range(4):
                    ins = v.tensor_scalar(area_d[:, k + j, t * P:(t + 1) * P],
                                          psum[:, g, j * P:(j + 1) * P], ln_chan[:, 0, k + j:k + j + 1],
                                          ln_chan[:, 1, k + j:k + j + 1], ALU.mult, ALU.add)
                ins.then_inc(h_cm_ready[0], 1)

            for g in (0, 2, 3, 4):
                input_plain(g)
            tiles = slice(UNIT // 2, UNIT)
            dve.wait_ge(high_ready, 1)
            v.tensor_tensor(w_part[0][1][:, tiles], raw_unit(0)[:, tiles], w_part[0][0][:, tiles].bitcast(F32),
                            ALU.subtract).then_inc(first_low, 1)
            input_low(0)
            for g in (6, 7):
                input_plain(g)
            for q in range(1, GROUPS):
                input_low(q)
            scale_shift(h0_ready)

            def low(n):
                u = UNITS * n + UNITS - 1
                dve.wait_ge(high_ready, u + 1)
                high, rest = w_part[u % SPLITS]
                v.tensor_tensor(rest[:], raw_unit(u), high[:].bitcast(F32), ALU.subtract).then_inc(dve_low, 1)

            def glu_product():
                dve.wait_ge(drained[0], 1)
                dve.wait_ge(drained[1], 1)
                dve.wait_ge(consts, CONSTS)
                dve.wait_ge(extra_drained, 3)
                link(v.tensor_tensor(glu[:, :, PAD_C:], plain, sigm, ALU.mult))

            def conv_c_taps(first, end):
                for k in range(first, end):
                    for c in range(CT):
                        if k >= 1:
                            dve.wait_ge(conv_c_step, (k - 1) * CT + c + 1)
                        tap = chan[:, c, k:k + 1]
                        src = glu[:, c, k:k + SEQ]
                        if k == 0:
                            ins = v.tensor_scalar(yc[:, c, :], src, tap, chan[:, c, TAPS_C:TAPS_C + 1],
                                                  ALU.mult, ALU.add)
                        else:
                            ins = v.scalar_tensor_tensor(out=yc[:, c, :], in0=src, scalar=tap, in1=yc[:, c, :],
                                                         op0=ALU.mult, op1=ALU.add)
                        ins.then_inc(conv_c_step, 1)

            v_ps = chunk_psum(2)

            def v_statistics():
                dve.wait_ge(units_done, 3 * UNITS)
                for t in range(TT):
                    link(v.bn_stats(v_stats[:, t, :], v_ps[:, t, :]))
                    link(v.bn_aggr(mv[:, t, :], v_stats[:, t:t + 1, :]))
                variance(slice(0, TT))

            def v_normalise():
                inverse_root(3, slice(0, TT))
                link(v.tensor_scalar(v_tm[:, 0, :], v_ps[:, 0, :], mv[:, 0, 0:1], rstd[:, 0, 2:3],
                                     ALU.subtract, ALU.mult))
                v.tensor_scalar(v_tm[:, 1, :], v_ps[:, 1, :], mv[:, 1, 0:1], rstd[:, 1, 2:3],
                                ALU.subtract, ALU.mult).then_inc(drained[2], 1)
                dve.wait_ge(drained[2], 1)
                dve.wait_ge(s_vrow, 16 * 4)
                link(v.tensor_tensor(v_tm, v_tm, v_rows[:, 0:1, :].to_broadcast([P, TT, CW]), ALU.mult))
                v.tensor_tensor(v_tm, v_tm, v_rows[:, 1:2, :].to_broadcast([P, TT, CW]),
                                ALU.add).then_inc(vn_ready, 1)

            def gate_b():
                dve.wait_ge(z_ready, 1)
                z = psum[:, 6:8, :].rearrange("p b (h s) -> p (b h) s", s=SEQ)
                link(v.tensor_tensor(work[:, :, 0:P], z[:, :, 0:P], gate_shift, ALU.add))
                v.tensor_tensor(work[:, :, P:SEQ], z[:, :, P:SEQ], gate_shift, ALU.add).then_inc(z_used, 1)
                dve.wait_ge(z_used, 1)
                dve.wait_ge(drained[0], 2)
                v.tensor_tensor(area_d[:, 8:12, :], work, u_cm, ALU.mult).then_inc(y_b_done, 1)

            def norm_c_difference():
                dve.wait_ge(c_mean, 1)
                mean = psum[:, 6:7, 0:SEQ].to_broadcast([P, CT, SEQ])
                link(v.tensor_tensor(yc, yc, mean, ALU.subtract))
                v.tensor_tensor(sigm, yc, yc, ALU.mult).then_inc(c_sq, 1)

            def norm_c():
                dve.wait_ge(c_var, 1)
                v.tensor_scalar(c_rstd[:, 0, :], psum[:, 7, 0:SEQ], EPS, None, ALU.add).then_inc(c_varused, 1)
                dve.wait_ge(root_ready, 4)
                link(v.reciprocal(c_rstd[:, 0, :], c_rstd[:, 1, :]))
                v.tensor_tensor(yc, yc, c_rstd[:, 0:1, :].to_broadcast([P, CT, SEQ]), ALU.mult).then_inc(c_norm, 1)

            def router_weights():
                dve.wait_ge(s_rt, 16)
                for dst, r in ((w_scaled, 2), (w_rt, 3)):
                    by = ln_chan[:, r, :].unsqueeze(2).to_broadcast([P, KT, E])
                    link(v.tensor_tensor(dst, w_rt, by, ALU.mult))
                link(v.tensor_reduce(w_sums[:, 0, :], w_scaled.rearrange("p k e -> p e k"), AX_X, ALU.add))
                v.tensor_reduce(w_sums[:, 1, :], w_rt.rearrange("p k e -> p e k"), AX_X,
                                ALU.add).then_inc(w_sums_ready, 1)

            def conv_a_half(a):
                n = N_FIRST + 3 * a
                dve.wait_ge(units_done, UNITS * (n + 2))
                dve.wait_ge(drained[1], 2 + a)
                v.tensor_tensor(gated_x[:, :, PAD_A:], plain, channel_psum(n + 1), ALU.mult).then_inc(drained[2], 1)
                dve.wait_ge(drained[2], 2 + a)
                dve.wait_ge(y_b_done, 1)
                first = CT * TAPS_A * a
                for k in range(TAPS_A):
                    for c in range(CT):
                        if k >= 1:
                            dve.wait_ge(conv_step, first + (k - 1) * CT + c + 1)
                        tap = chan[:, c, ROW_A + TAPS_A * a + k:ROW_A + TAPS_A * a + k + 1]
                        src = gated_x[:, c, k:k + SEQ]
                        if k == 0:
                            ins = v.tensor_scalar(work[:, c, :], src, tap, None, ALU.mult)
                        else:
                            ins = v.scalar_tensor_tensor(out=work[:, c, :], in0=src, scalar=tap, in1=work[:, c, :],
                                                         op0=ALU.mult, op1=ALU.add)
                        ins.then_inc(conv_step, 1)
                dve.wait_ge(conv_step, first + CT * TAPS_A)

            def gate_a(a):
                n = N_FIRST + 3 * a + 2
                dve.wait_ge(units_done, UNITS * (n + 1))
                v.tensor_tensor(area_d[:, CT * a:CT * (a + 1), :], work, channel_psum(n),
                                ALU.mult).then_inc(drained[0], 1)

            def low_output(q):
                dve.wait_ge(in_high, TT * KT // 4 + q + 1)
                tiles = slice(4 * q, 4 * q + 4)
                v.tensor_tensor(in_part[1][:, tiles, :], area_d[:, tiles, :], in_part[0][:, tiles, :].bitcast(F32),
                                ALU.subtract).then_inc(in_low, 1)

            def residual(n):
                dve.wait_ge(units_done, UNITS * (n + 1))
                cols = slice((n - N_IN) * CW, (n - N_IN + 1) * CW)
                for t in range(TT):
                    ins = v.scalar_tensor_tensor(out=area_a[:, t, cols], in0=area_b[:, t, cols], scalar=ALPHA,
                                                 in1=chunk_psum(n)[:, t, :], op0=ALU.mult, op1=ALU.add)
                    if t < TT - 1:
                        link(ins)
                ins.then_inc(drained[n % 3], 1)
                dve.wait_ge(drained[n % 3], n // 3 + 1)
                for t in range(TT):
                    link(v.bn_stats(stats[:, t, n - N_IN, :], area_a[:, t, cols]))

            low(0)
            low(1)
            low(2)
            glu_product()
            conv_c_taps(0, 10)
            low(3)
            v_statistics()
            conv_c_taps(10, 12)
            v_normalise()
            conv_c_taps(12, 16)
            low(4)
            conv_c_taps(16, 23)
            low(5)
            gate_b()
            conv_c_taps(23, TAPS_C)
            low(6)
            conv_a_half(0)
            norm_c_difference()
            low(7)
            gate_a(0)
            low(8)
            norm_c()
            router_weights()
            low(9)
            conv_a_half(1)
            dve.wait_ge(units_done, UNITS * N_IN)
            low_output(0)
            gate_a(1)
            for q in range(1, UNITS):
                low_output(q)
            low(10)
            for n in range(N_IN, N_MIX):
                if n < N_MIX - 1:
                    low(n + 1)
                residual(n)

            for t in range(TT):
                link(v.bn_aggr(mv[:, t, :], stats[:, t]))
            variance(slice(0, TT))
            norm_scale(5, slice(0, TT))
            dve.wait_ge(scale_ready, TT * 2)

            def tile(n):
                return rt[:, n, :]

            def t2(ap, w=E):
                return ap.rearrange("p (t e) -> p t e", t=TT)

            probs, sel, val, pick1, pick2, picks, tmp, small = (tile(n) for n in range(8))
            dve.wait_ge(rows_kept, 1)
            for t in range(TT):
                link(v.scalar_tensor_tensor(out=logit_bias[:, t * E:(t + 1) * E], in0=logit_rows[:, 0, :],
                                            scalar=rstd[:, t, 3:4], in1=logit_rows[:, 1, :],
                                            op0=ALU.mult, op1=ALU.add))
            dve.wait_ge(logits_ready, 1)
            for t in range(TT):
                ins = v.scalar_tensor_tensor(out=small[:, t * E:(t + 1) * E], in0=psum[:, 4, t * E:(t + 1) * E],
                                             scalar=rstd[:, t, 2:3], in1=logit_bias[:, t * E:(t + 1) * E],
                                             op0=ALU.mult, op1=ALU.add)
                if t < TT - 1:
                    link(ins)
            ins.then_inc(logits_fixed, 1)
            dve.wait_ge(probs_ready, 1)
            link(v.tensor_tensor(t2(sel), t2(probs), b_rt[:].unsqueeze(1).to_broadcast([P, TT, E]), ALU.add))
            s4 = sel.rearrange("p (g e) -> p g e", e=GE)
            q = tmp.rearrange("p (n g) -> p n g", n=4)
            r = small.rearrange("p (n g) -> p n g", n=4)
            link(v.tensor_tensor(q[:, 0, :], s4[:, :, 0], s4[:, :, 1], ALU.max))
            link(v.tensor_tensor(q[:, 1, :], s4[:, :, 2], s4[:, :, 3], ALU.max))
            link(v.tensor_tensor(q[:, 2, :], s4[:, :, 0], s4[:, :, 1], ALU.min))
            link(v.tensor_tensor(q[:, 3, :], s4[:, :, 2], s4[:, :, 3], ALU.min))
            link(v.tensor_tensor(r[:, 0, :], q[:, 0, :], q[:, 1, :], ALU.max))
            link(v.tensor_tensor(r[:, 1, :], q[:, 0, :], q[:, 1, :], ALU.min))
            link(v.tensor_tensor(r[:, 2, :], q[:, 2, :], q[:, 3, :], ALU.max))
            link(v.tensor_tensor(r[:, 3, :], r[:, 1, :], r[:, 2, :], ALU.max))
            link(v.tensor_tensor(q[:, 0, :], r[:, 0, :], r[:, 3, :], ALU.add))

            best = rstd[:, :, 0]

            def first_largest(dst, scores, key, width, scratch):
                s3 = scores.rearrange("p (t e) -> p t e", t=TT)
                d3 = dst.rearrange("p (t e) -> p t e", t=TT)
                c3 = scratch.rearrange("p (t e) -> p t e", t=TT)
                wide = [P, TT, width]
                link(v.tensor_reduce(best, s3, AX_X, ALU.max))
                link(v.tensor_tensor(c3, s3, best.unsqueeze(2).to_broadcast(wide), ALU.is_equal))
                link(v.tensor_tensor(c3, c3, key, ALU.mult))
                link(v.tensor_reduce(best, c3, AX_X, ALU.max))
                link(v.tensor_tensor(d3, c3, best.unsqueeze(2).to_broadcast(wide), ALU.is_equal))

            first_largest(q[:, 1, :], q[:, 0, :], group_key[:], NG, q[:, 2, :])
            link(v.tensor_scalar(q[:, 3, :], q[:, 1, :], FAR, -FAR, ALU.mult, ALU.add))
            v4 = val.rearrange("p (g e) -> p g e", e=GE)
            wide = [P, TT * NG, GE]
            link(v.tensor_tensor(v4, s4, q[:, 1, :].unsqueeze(2).to_broadcast(wide), ALU.mult))
            link(v.tensor_tensor(v4, v4, q[:, 3, :].unsqueeze(2).to_broadcast(wide), ALU.add))
            first_largest(pick1, val, expert_key[:], E, tmp)
            link(v.scalar_tensor_tensor(out=val, in0=pick1, scalar=-2 * FAR, in1=val, op0=ALU.mult, op1=ALU.add))
            first_largest(pick2, val, expert_key[:], E, tmp)
            v.tensor_tensor(picks, pick1, pick2, ALU.add).then_inc(picks_ready, 1)
            dve.wait_ge(ranks_ready, 1)
            link(v.scalar_tensor_tensor(out=tmp, in0=psum[:, 1, 0:TT * E], scalar=1.0, in1=picks,
                                        op0=ALU.add, op1=ALU.mult))

            def block_ranks(b):
                link(v.tensor_scalar(rank[:, :, b * E:(b + 1) * E], t2(tmp), -1.0 - CAP * b, None, ALU.add))

            def place(it):
                now = rank[:, :, bass.ds(2 * it, 2)].unsqueeze(3).to_broadcast([P, TT, 2, CAP])
                v.tensor_tensor(one_hot[:], slot_no[:].rearrange("p (t i) s -> p t i s", t=TT), now,
                                ALU.is_equal).then_inc(onehot_ready, 1)

            link(v.tensor_reduce(best[:, 0:1], psum[:, 1, 2 * E:3 * E], AX_X, ALU.max))
            block_ranks(0)
            place(0)
            for b in range(1, BLOCKS + 1):
                block_ranks(b)
            v.tensor_scalar(overflow[:], best[:, 0:1], float(CAP), None, ALU.is_gt).then_inc(flag_ready, 1)
            dve.wait_ge(normed, 2 * TT * 2)
            sums = rstd
            for i, pick in enumerate((pick1, pick2)):
                link(v.tensor_tensor(tmp, pick, probs, ALU.mult))
                link(v.tensor_reduce(sums[:, :, 1 + i], t2(tmp), AX_X, ALU.add))
            link(v.tensor_tensor(best, sums[:, :, 1], sums[:, :, 2], ALU.add))
            link(v.reciprocal(best, best))
            for i, pick in enumerate((pick1, pick2)):
                link(v.tensor_tensor(sums[:, :, 1 + i], sums[:, :, 1 + i], best, ALU.mult))
                link(v.tensor_tensor(t2(pick), t2(pick), sums[:, :, 1 + i].unsqueeze(2).to_broadcast([P, TT, E]),
                                     ALU.mult))
            for b in range(BLOCKS + 1):
                link(v.tensor_tensor(gate[:, :, b * E:(b + 1) * E], t2(pick1), t2(pick2), ALU.add))
            def step(it):
                dve.wait_ge(onehot_ready, it + 1)
                now = gate[:, :, bass.ds(2 * it, 2)].unsqueeze(3).to_broadcast([P, TT, 2, CAP])
                v.tensor_tensor(one_hot_g[:], one_hot[:], now, ALU.mult).then_inc(gated_ready, 1)
                dve.wait_ge(gather_ready, 4 * it + 4)
                dve.wait_ge(gated_ready, it + 1)
                place(it + 1)
                dve.wait_ge(silu_ready, it + 1)
                dve.wait_ge(experts_done, STEP_UNITS * it + 2 * UNITS)
                v.tensor_tensor(hidden, silu_h, psum[:, 1, :], ALU.mult).then_inc(hidden_ready, 1)
                for c in range(NC):
                    dve.wait_ge(comb_ready, 4 * it + c + 1)
                    cols = slice(c * CW, (c + 1) * CW)
                    v.tensor_tensor(area_a[:, 0, cols], area_a[:, 0, cols], psum[:, 6, :], ALU.add)
                    v.tensor_tensor(area_a[:, 1, cols], area_a[:, 1, cols], psum[:, 7, :],
                                    ALU.add).then_inc(comb_added, 1)
                    dve.wait_ge(comb_added, 4 * it + c + 1)
                    v.bn_stats(stats[:, 0, c, :], area_a[:, 0, cols])
                    v.bn_stats(stats[:, 1, c, :], area_a[:, 1, cols]).then_inc(stats_done, 1)

            dve.wait_ge(s_g, 32 * 2)
            for t in range(TT):
                for h in range(2):
                    cols = slice(h * D // 2, (h + 1) * D // 2)
                    link(v.scalar_tensor_tensor(out=area_a[:, t, cols], in0=area_b[:, t, cols], scalar=ALPHA,
                                                in1=area_g[:, 0, cols], op0=ALU.mult, op1=ALU.mult))
                    v.scalar_tensor_tensor(out=area_a[:, t, cols], in0=area_g[:, 1, cols], scalar=ALPHA,
                                           in1=area_a[:, t, cols], op0=ALU.mult, op1=ALU.add).then_inc(x1_ready, 1)
            dve.wait_ge(x1_ready, 2 * TT)
            with dve.Fori(0, PAIRS) as it:
                step(it)
            dve.wait_ge(stats_done, NC * PAIRS)
            more = dve.value_load(overflow[0:1, 0:1], min_val=0, max_val=1)
            with dve.If(more > 0):
                with dve.Fori(PAIRS, BLOCKS * PAIRS) as it:
                    step(it)
                dve.wait_ge(stats_done, NC * PAIRS * BLOCKS)
            with dve.Else():
                dve.nop()

            for t in range(TT):
                link(v.bn_aggr(mv[:, t, :], stats[:, t]))
            variance(slice(0, TT))
            dve.wait_ge(s_g2, 16 * 3)
            for m in range(2 * TT - 1):
                t, h = divmod(m, 2)
                cols = slice(h * D // 2, (h + 1) * D // 2)
                link(v.scalar_tensor_tensor(out=area_b[:, t, cols], in0=area_a[:, t, cols], scalar=mv[:, t, 0:1],
                                            in1=ln2_scale[:, cols], op0=ALU.subtract, op1=ALU.mult))
                if m == 0:
                    norm_scale(6, slice(0, TT))
                v.scalar_tensor_tensor(out=area_b[:, t, cols], in0=area_b[:, t, cols], scalar=rstd[:, t, 2:3],
                                       in1=ln2_shift[h], op0=ALU.mult, op1=ALU.add).then_inc(y_out, 1)


_INS = ["x", "ln_in_g", "ln_in_b", "w_in", "conv_a", "gate_ws", "gate_bs", "ln_v_g", "ln_v_b", "conv_c",
        "conv_c_b", "ln_c_g", "ln_c_b", "w_out", "ln1_g", "ln1_b", "w_router", "b_router", "w1", "w3", "w2",
        "ln2_g", "ln2_b"]


def kernel(**inputs):
    import numpy as _np
    import concourse.bacc as _bacc
    from concourse import mybir as _mybir
    from concourse.bass_utils import run_bass_kernel_spmd as _run

    nc = _bacc.Bacc("TRN2", target_bir_lowering=False, num_devices=1)
    arrays, args = {}, []
    for name in _INS:
        a = _np.ascontiguousarray(inputs[name])
        arrays[f"in_{name}_dram"] = a
        args.append(nc.dram_tensor(f"in_{name}_dram", a.shape, _mybir.dt.from_np(a.dtype), kind="ExternalInput").ap())
    shape = inputs["x"].shape
    args.append(nc.dram_tensor("out_0_dram", shape, _mybir.dt.float32, kind="ExternalOutput").ap())
    hybrid_layer(nc, *args)
    r = _run(nc, [arrays], core_ids=[0])
    return r.results[0]["out_0_dram"]
```
